# Optimizing a Trainium2 kernel written in Bass

```python
import jax, jax.numpy as jnp
from jax import lax
import numpy as np

D_MODEL = 1024
BATCH = 1
SEQ = 1024
DEPTH = 2

GRID_W = 64
CTX_LEN = 256
N_HEADS = 8
QK_NOPE_DIM = 64
QK_ROPE_DIM = 32
QK_HEAD_DIM = QK_NOPE_DIM + QK_ROPE_DIM
V_HEAD_DIM = 64
Q_LORA_RANK = 256
KV_LORA_RANK = 128
MLA_WIDTH = N_HEADS * V_HEAD_DIM
ROPE_AXIS_DIM = QK_ROPE_DIM // 2
ROPE_BASE = 10000.0
Q_BLOCK = 128
FOURIER_GROUPS = 4
FOURIER_GROUP_DIM = 128
FOURIER_WIDTH = FOURIER_GROUPS * FOURIER_GROUP_DIM
MIX_WIDTH = MLA_WIDTH + FOURIER_WIDTH
IN_PROJ_WIDTH = Q_LORA_RANK + KV_LORA_RANK + QK_ROPE_DIM + FOURIER_WIDTH
N_EXPERTS = 16
N_EXPERT_GROUPS = 4
EXPERTS_PER_GROUP = N_EXPERTS // N_EXPERT_GROUPS
TOP_K = 2
D_EXPERT = 256
EXPERT_BLOCK = 128
EPS = 1e-6

kernel_name = "hymba_mla_fnet_grouped_moe_dit"

def rms_norm(x, g):
    xf = x.astype(jnp.float32)
    y = xf * lax.rsqrt(jnp.mean(xf * xf, axis=-1, keepdims=True) + EPS)
    return (y * g.astype(jnp.float32)).astype(x.dtype)

def modulate(h, shift, scale):
    return h * (1 + scale) + shift

def grid_angles(n_lat):
    rows = n_lat // GRID_W
    row = jnp.repeat(jnp.arange(rows, dtype=jnp.float32), GRID_W)
    col = jnp.tile(jnp.arange(GRID_W, dtype=jnp.float32), rows)
    half = ROPE_AXIS_DIM // 2
    freqs = ROPE_BASE ** (-jnp.arange(half, dtype=jnp.float32) / half)
    return row[:, None] * freqs, col[:, None] * freqs

def rope_1d(x, ang):
    f = x.shape[-1] // 2
    cos = jnp.cos(ang)[None, :, None, :].astype(x.dtype)
    sin = jnp.sin(ang)[None, :, None, :].astype(x.dtype)
    x1, x2 = x[..., :f], x[..., f:]
    return jnp.concatenate([x1 * cos - x2 * sin, x2 * cos + x1 * sin], axis=-1)

def rope_tail_2d(t, ang_row, ang_col):
    nope, rp = t[..., :QK_NOPE_DIM], t[..., QK_NOPE_DIM:]
    rp = jnp.concatenate([rope_1d(rp[..., :ROPE_AXIS_DIM], ang_row),
                          rope_1d(rp[..., ROPE_AXIS_DIM:], ang_col)], axis=-1)
    return jnp.concatenate([nope, rp], axis=-1)

def mla_queries(cq, q_a_norm, w_q_b, q_norm, ang_row, ang_col):
    B, N, _ = cq.shape
    q = (rms_norm(cq, q_a_norm) @ w_q_b).reshape(B, N, N_HEADS, QK_HEAD_DIM)
    q = rms_norm(q, q_norm)
    if ang_row is not None:
        q = rope_tail_2d(q, ang_row, ang_col)
    return q

def mla_keys_values(ckv, k_rope, kv_a_norm, w_kv_b, k_norm, ang_row, ang_col):
    B, N, _ = ckv.shape
    kv = (rms_norm(ckv, kv_a_norm) @ w_kv_b).reshape(B, N, N_HEADS, QK_NOPE_DIM + V_HEAD_DIM)
    k_nope, v = kv[..., :QK_NOPE_DIM], kv[..., QK_NOPE_DIM:]
    k_r = jnp.broadcast_to(k_rope[:, :, None, :], (B, N, N_HEADS, QK_ROPE_DIM))
    k = rms_norm(jnp.concatenate([k_nope, k_r], axis=-1), k_norm)
    if ang_row is not None:
        k = rope_tail_2d(k, ang_row, ang_col)
    return k, v

def blocked_attention(q, k, v):
    B, Nq, H, Dq = q.shape
    nb = Nq // Q_BLOCK
    qb = q.reshape(B, nb, Q_BLOCK, H, Dq).transpose(1, 0, 2, 3, 4)
    kt = k.transpose(0, 2, 1, 3)
    vt = v.transpose(0, 2, 1, 3)
    scale = QK_HEAD_DIM ** -0.5

    def one_block(qblk):
        s = jnp.einsum('bqhd,bhkd->bhqk', qblk, kt).astype(jnp.float32) * scale
        p = jax.nn.softmax(s, axis=-1).astype(vt.dtype)
        return jnp.einsum('bhqk,bhkd->bqhd', p, vt)

    o = lax.map(one_block, qb)
    return o.transpose(1, 0, 2, 3, 4).reshape(B, Nq, H * V_HEAD_DIM)

def fourier_mix(f, w_fourier):
    B, N, _ = f.shape
    z = f.reshape(B, N, FOURIER_GROUPS, FOURIER_GROUP_DIM).astype(jnp.float32)
    zr = jnp.fft.fft2(z, axes=(1, 3), norm="ortho").real.astype(f.dtype)
    return jnp.einsum('bngc,gcd->bngd', zr, w_fourier).reshape(B, N, FOURIER_WIDTH)

def hybrid_mixer(h_ctx, h_lat, ang_row, ang_col, w_in, q_a_norm, w_q_b, kv_a_norm, w_kv_b,
                 q_norm, k_norm, w_fourier, w_out, with_ctx_out):
    cuts = [Q_LORA_RANK, Q_LORA_RANK + KV_LORA_RANK, Q_LORA_RANK + KV_LORA_RANK + QK_ROPE_DIM]
    cq_c, ckv_c, kr_c, f_c = jnp.split(h_ctx @ w_in, cuts, axis=-1)
    cq_l, ckv_l, kr_l, f_l = jnp.split(h_lat @ w_in, cuts, axis=-1)
    k_c, v_c = mla_keys_values(ckv_c, kr_c, kv_a_norm, w_kv_b, k_norm, None, None)
    k_l, v_l = mla_keys_values(ckv_l, kr_l, kv_a_norm, w_kv_b, k_norm, ang_row, ang_col)
    k_all = jnp.concatenate([k_c, k_l], axis=1)
    v_all = jnp.concatenate([v_c, v_l], axis=1)
    q_l = mla_queries(cq_l, q_a_norm, w_q_b, q_norm, ang_row, ang_col)
    o_lat = blocked_attention(q_l, k_all, v_all)
    out_lat = jnp.concatenate([o_lat, fourier_mix(f_l, w_fourier)], axis=-1) @ w_out
    out_ctx = None
    if with_ctx_out:
        q_c = mla_queries(cq_c, q_a_norm, w_q_b, q_norm, None, None)
        o_ctx = blocked_attention(q_c, k_c, v_c)
        out_ctx = jnp.concatenate([o_ctx, fourier_mix(f_c, w_fourier)], axis=-1) @ w_out
    return out_ctx, out_lat

def grouped_moe(h, router_w, router_bias, w_gate, w_up, w_down):
    T, D = h.shape
    scores = jax.nn.sigmoid((h @ router_w).astype(jnp.float32))
    biased = (scores + router_bias.astype(jnp.float32)).reshape(T, N_EXPERT_GROUPS, EXPERTS_PER_GROUP)
    group_score = lax.top_k(biased, TOP_K)[0].sum(-1)
    grp = jnp.argmax(group_score, axis=-1).astype(jnp.int32)
    in_grp = jnp.take_along_axis(biased, grp[:, None, None], axis=1)[:, 0]
    _, local = lax.top_k(in_grp, TOP_K)
    expert = grp[:, None] * EXPERTS_PER_GROUP + local.astype(jnp.int32)
    wts = jnp.take_along_axis(scores, expert, axis=1)
    wts = wts / jnp.sum(wts, axis=-1, keepdims=True)
    A = T * TOP_K
    e = expert.reshape(A)
    tok = jnp.repeat(jnp.arange(T, dtype=jnp.int32), TOP_K)
    w = wts.reshape(A)
    order = jnp.argsort(e)
    e_s, tok_s, w_s = e[order], tok[order], w[order]
    counts = jnp.zeros((N_EXPERTS,), jnp.int32).at[e].add(1)
    padded = (counts + EXPERT_BLOCK - 1) // EXPERT_BLOCK * EXPERT_BLOCK
    pad_end = jnp.cumsum(padded)
    pad_start = pad_end - padded
    raw_start = jnp.cumsum(counts) - counts
    dest = pad_start[e_s] + jnp.arange(A, dtype=jnp.int32) - raw_start[e_s]
    n_blocks = -(-A // EXPERT_BLOCK) + N_EXPERTS
    P = n_blocks * EXPERT_BLOCK
    buf_tok = jnp.zeros((P,), jnp.int32).at[dest].set(tok_s)
    xb = h[buf_tok].reshape(n_blocks, EXPERT_BLOCK, D)
    blk_start = jnp.arange(n_blocks, dtype=jnp.int32) * EXPERT_BLOCK
    blk_e = jnp.minimum(jnp.searchsorted(pad_end, blk_start, side='right'), N_EXPERTS - 1)

    def expert_block(args):
        xblk, ei = args
        return (jax.nn.silu(xblk @ w_gate[ei]) * (xblk @ w_up[ei])) @ w_down[ei]

    yb = lax.map(expert_block, (xb, blk_e)).reshape(P, D)
    y = yb[dest] * w_s[:, None].astype(h.dtype)
    return jnp.zeros_like(h).at[tok_s].add(y)

def setup_inputs(seed: int = 0) -> dict:
    key = jax.random.key(seed)
    ks = jax.random.split(key, 24)
    D, L, E = D_MODEL, DEPTH, N_EXPERTS
    nrm = lambda k, shape, fan_in: jax.random.normal(k, shape, jnp.float32) * fan_in ** -0.5
    gain = lambda k, shape: 1.0 + 0.02 * jax.random.normal(k, shape, jnp.float32)
    return {
        "x": jax.random.normal(ks[0], (BATCH, SEQ, D), jnp.float32),
        "c": jax.random.normal(ks[1], (BATCH, D), jnp.float32),
        "ctx": jax.random.normal(ks[2], (BATCH, CTX_LEN, D), jnp.float32),
        "c_ctx": jax.random.normal(ks[3], (D,), jnp.float32),
        "w_ada": nrm(ks[4], (L, D, 6 * D), D) * 0.5,
        "b_ada": 0.01 * jax.random.normal(ks[5], (L, 6 * D), jnp.float32),
        "norm_mix": gain(ks[6], (L, D)),
        "norm_ffn": gain(ks[7], (L, D)),
        "w_in": nrm(ks[8], (L, D, IN_PROJ_WIDTH), D),
        "q_a_norm": gain(ks[9], (L, Q_LORA_RANK)),
        "w_q_b": nrm(ks[10], (L, Q_LORA_RANK, N_HEADS * QK_HEAD_DIM), Q_LORA_RANK),
        "kv_a_norm": gain(ks[11], (L, KV_LORA_RANK)),
        "w_kv_b": nrm(ks[12], (L, KV_LORA_RANK, N_HEADS * (QK_NOPE_DIM + V_HEAD_DIM)), KV_LORA_RANK),
        "q_norm": gain(ks[13], (L, QK_HEAD_DIM)),
        "k_norm": gain(ks[14], (L, QK_HEAD_DIM)),
        "w_fourier": nrm(ks[15], (L, FOURIER_GROUPS, FOURIER_GROUP_DIM, FOURIER_GROUP_DIM), FOURIER_GROUP_DIM),
        "w_out": nrm(ks[16], (L, MIX_WIDTH, D), MIX_WIDTH),
        "router_w": nrm(ks[17], (D, E), D),
        "router_bias": 0.01 * jax.random.normal(ks[18], (E,), jnp.float32),
        "w_gate": nrm(ks[19], (L, E, D, D_EXPERT), D),
        "w_up": nrm(ks[20], (L, E, D, D_EXPERT), D),
        "w_down": nrm(ks[21], (L, E, D_EXPERT, D), D_EXPERT),
    }

def reference(x, c, ctx, c_ctx, w_ada, b_ada, norm_mix, norm_ffn, w_in, q_a_norm, w_q_b,
              kv_a_norm, w_kv_b, q_norm, k_norm, w_fourier, w_out, router_w, router_bias,
              w_gate, w_up, w_down):
    B, S, D = x.shape
    n_ctx = ctx.shape[1]
    ang_row, ang_col = grid_angles(S)
    for l in range(DEPTH):
        last = l == DEPTH - 1
        mod_lat = (jax.nn.silu(c) @ w_ada[l] + b_ada[l])[:, None, :]
        mod_ctx = jax.nn.silu(c_ctx) @ w_ada[l] + b_ada[l]
        sh1, sc1, g1, sh2, sc2, g2 = jnp.split(mod_lat, 6, axis=-1)
        csh1, csc1, cg1, csh2, csc2, cg2 = jnp.split(mod_ctx, 6, axis=-1)
        h_lat = modulate(rms_norm(x, norm_mix[l]), sh1, sc1)
        h_ctx = modulate(rms_norm(ctx, norm_mix[l]), csh1, csc1)
        mix_ctx, mix_lat = hybrid_mixer(h_ctx, h_lat, ang_row, ang_col, w_in[l], q_a_norm[l], w_q_b[l],
                                        kv_a_norm[l], w_kv_b[l], q_norm[l], k_norm[l], w_fourier[l],
                                        w_out[l], not last)
        x = x + g1 * mix_lat
        f_lat = modulate(rms_norm(x, norm_ffn[l]), sh2, sc2).reshape(B * S, D)
        if last:
            y = grouped_moe(f_lat, router_w, router_bias, w_gate[l], w_up[l], w_down[l])
            x = x + g2 * y.reshape(B, S, D)
        else:
            ctx = ctx + cg1 * mix_ctx
            f_ctx = modulate(rms_norm(ctx, norm_ffn[l]), csh2, csc2).reshape(B * n_ctx, D)
            y = grouped_moe(jnp.concatenate([f_ctx, f_lat], axis=0), router_w, router_bias,
                            w_gate[l], w_up[l], w_down[l])
            ctx = ctx + cg2 * y[:B * n_ctx].reshape(B, n_ctx, D)
            x = x + g2 * y[B * n_ctx:].reshape(B, S, D)
    return x


_drawn_inputs = setup_inputs


def setup_inputs(seed=0):
    import zlib

    import numpy as np

    out = dict(_drawn_inputs(seed))
    spreads = {}
    factors = {'ctx': 3.375,
     'norm_mix': 3.587,
     'q_a_norm': 8.0,
     'kv_a_norm': 4.187,
     'q_norm': 8.0,
     'k_norm': 8.0}
    for name, (base, spread) in spreads.items():
        noise = np.random.default_rng([zlib.crc32(name.encode()), seed]).standard_normal(out[name].shape)
        drawn = base * np.exp(spread * noise) if base else spread * noise
        out[name] = __import__('jax').numpy.asarray(drawn.astype(out[name].dtype))
    for name, factor in factors.items():
        out[name] = (out[name] * factor).astype(out[name].dtype)
    return out
```

```python
from contextlib import ExitStack

import numpy as np

import concourse.bass as bass
from concourse import mybir

P = 128
D = 1024
KD = D // P
SEQ, CTX = 1024, 256
LAT_TILES, CTX_TILES = SEQ // P, CTX // P
TILES = CTX_TILES + LAT_TILES
TOK = TILES * P
DEPTH = 2
HEADS, NOPE, ROPE, VDIM = 8, 64, 32, 64
QK = NOPE + ROPE
QR, KVR = 256, 128
CW = QR + KVR + ROPE
FG, FD = 4, 128
FW = FG * FD
INW = CW + FW
GRID_W = 64
NE, NG, EPG, DE = 16, 4, 4, 256
EPS = 1e-6
SCALE = float(QK) ** -0.5
WSLOT = KD * 2 * DE + (DE // P) * D
BIG = 1e30

F32 = mybir.dt.float32
I32 = mybir.dt.int32
ALU = mybir.AluOpType
ACT = mybir.ActivationFunctionType
AX = mybir.AxisListType.X

_W = dict(ident=P, tri=P, ones=P, tw=5 * 3 * P, cc=P, nsc=P, rc=TILES * ROPE, rs=TILES * ROPE,
          prio=NE, prio4=NG, sign=2, iota=P, tok=TILES)
_AT, _n = {}, 0
for _k, _v in _W.items():
    _AT[_k] = (_n, _n + _v)
    _n += _v
CST_W = _n


def constant_tile():
    c = np.zeros((P, CST_W), np.float64)

    def put(name, a):
        c[:, _AT[name][0]:_AT[name][1]] = a

    p = np.arange(P)
    put("ident", np.eye(P))
    put("tri", (p[:, None] < p[None, :]) * 1.0)
    put("ones", 1.0)
    tw = np.zeros((P, 5, 3, P))
    for r in range(5):
        a = 2 * np.pi * ((p[:, None] * (8 * p[None, :] + r)) % SEQ) / SEQ
        tw[:, r, 0], tw[:, r, 1], tw[:, r, 2] = -np.sin(a), np.cos(a), np.sin(a)
    put("tw", tw.reshape(P, -1))
    a = 2 * np.pi * ((p[:, None] * p[None, :]) % FD) / FD
    s = 1.0 / np.sqrt(SEQ * FD)
    put("cc", np.cos(a) * s)
    put("nsc", -np.sin(a) * s)
    half = ROPE // 4
    freqs = np.float32(10000.0) ** (-np.arange(half, dtype=np.float32) / np.float32(half))
    rc = np.ones((P, TILES, ROPE))
    rs = np.zeros((P, TILES, ROPE))
    for t in range(LAT_TILES):
        n = t * P + p
        for axis, pos in enumerate((n // GRID_W, n % GRID_W)):
            ang = (pos.astype(np.float32)[:, None] * freqs).astype(np.float64)
            o = axis * 2 * half
            rc[:, CTX_TILES + t, o:o + 2 * half] = np.tile(np.cos(ang), (1, 2))
            rs[:, CTX_TILES + t, o:o + half] = -np.sin(ang)
            rs[:, CTX_TILES + t, o + half:o + 2 * half] = np.sin(ang)
    put("rc", rc.reshape(P, -1))
    put("rs", rs.reshape(P, -1))
    put("prio", np.arange(NE, 0, -1))
    put("prio4", np.arange(NG, 0, -1))
    put("iota", np.arange(P))
    put("tok", np.arange(TILES)[None, :] * P + p[:, None])
    put("sign", [1.0, -1.0])
    return c.astype(np.float32)


def build_backbone(nc, x, c, ctx, c_ctx, w_ada, b_ada, norm_mix, norm_ffn, w_in, q_a_norm, w_q_b,
                   kv_a_norm, w_kv_b, q_norm, k_norm, w_fourier, w_out, router_w, router_bias,
                   w_gate, w_up, w_down, cst, out):
    es = ExitStack()
    with es:
        def sb(name, shape, dt=F32):
            return es.enter_context(nc.sbuf_tensor(name, shape, dt))

        def sem(name):
            return es.enter_context(nc.semaphore(name))

        def dram(name, shape, dt=F32):
            return nc.dram_tensor(name, shape, dt, kind="Internal").ap()

        rows_d = dram("rows_d", (DEPTH, 2, 6 * D))
        qT_d = dram("qT_d", (TILES, QK, HEADS * P))
        xmid_d = dram("xmid_d", (TOK, D))
        xnext_d = dram("xnext_d", (TOK, D))
        f_d = dram("f_d", (TOK, D))
        NBMAX = 2 * TOK // P + NE
        yb_d = dram("yb_d", (NBMAX * P, D))

        CST = sb("CST", [P, CST_W])

        def k(name, lo=0, hi=None):
            a, b = _AT[name]
            return CST[:, a + lo:(b if hi is None else a + hi)]

        ident = k("ident")
        KV = sb("KV", [P, 15360 + 13312])
        ZO = sb("ZO", [P, TILES * FW])
        R2 = sb("R2", [P, 11776])
        PR = sb("PR", [67, DEPTH, P])
        PCOL = sb("PCOL", [P, DEPTH, 67])
        CR = sb("CR", [KD, 2, P])
        CE = sb("CE", [KD, 2, P])
        SC = sb("SC", [P, KD, 2])
        MOD = sb("MOD", [P, DEPTH, 2, 48])
        ROWS = sb("ROWS", [96, P])
        GN = sb("GN", [P, DEPTH, 2, QK])
        WF = sb("WF", [P, FG * FD])
        FM = sb("FM", [P, 2, FG * FD])
        RW = sb("RW", [P, KD, NE])
        RB = sb("RB", [P, NE])
        EPSC = sb("EPSC", [P, 1])
        sm = sb("sm", [P, 64])
        EO = sb("EO", [1, NE], I32)
        FB = sb("FB", [1, NE], I32)
        BE = sb("BE", [1, NBMAX], I32)
        DST = sb("DST", [P, 2, TILES], I32)
        WT = sb("WT", [P, 2, TILES])
        IDS = sb("IDS", [P, NBMAX], I32)
        IDX = sb("IDX", [P, 4], I32)

        PS = es.enter_context(nc.psum_tensor("PS", [P, 8, 512], F32))

        def bank(b, lo=0, hi=512):
            return PS[:, b, lo:hi]

        R1 = KV[:, 15360:28672]
        kT = KV[:, 0:HEADS * TOK].rearrange("p (h n) -> p h n", h=HEADS)
        V = KV[:, 10240:15360]
        ADP = 6 * D // 512
        wada = [KV[:, 4096 * u:4096 * (u + 1)].rearrange("p (k n) -> p k n", k=KD) for u in range(3)]
        arow = [R2[0:2, 10240 + 512 * u:10752 + 512 * u] for u in range(3)]
        wslot = [KV[:, WSLOT * u:WSLOT * (u + 1)] for u in range(3)]
        rowsD = KV[:, 9216:15360].rearrange("p (s v n) -> p s v n", s=2, v=3)
        win = R1[:, 3328:3328 + KD * INW].rearrange("p (k n) -> p k n", k=KD)
        wqb = R1[:, 10752:12288].rearrange("p (k n) -> p k n", k=2)
        wkv = R1[:, 12288:13312]
        UV = R1[:, 0:8192].rearrange("p (z g n) -> p z g n", z=2, g=FG)
        FT = R1[:, 8192:13312].rearrange("p (g n) -> p g n", g=FG)
        wout = R1[:, 0:8192].rearrange("p (k n) -> p k n", k=KD)

        def take(sizes):
            o, views = 0, []
            for s in sizes:
                views.append(R2[:, o:o + s])
                o += s
            assert o <= 11776, o
            return views

        cst_in, cin, prm_in, gn_in = sem("cst_in"), sem("cin"), sem("prm_in"), sem("gn_in")
        cexp, csilu, cT_ps, sc_ready = sem("cexp"), sem("csilu"), sem("cT_ps"), sem("sc_ready")
        ada_in = [sem(f"ada_in{u}") for u in range(3)]
        arow_ready, arow_out, raw_in, raw_ps = sem("arow_ready"), [sem(f"arow_out{u}") for u in range(3)], sem("raw_in"), sem("raw_ps")
        ada_mm, mod_done, rows_ps, rows_ready, rows_out = (sem("ada_mm"), sem("mod_done"), sem("rows_ps"),
                                                           sem("rows_ready"), sem("rows_out"))
        prm_ps, prm_ready = sem("prm_ps"), sem("prm_ready")
        dst_ = sem("dve_step")
        ast_ = sem("act_step")
        pst_ = sem("pool_step")
        pool_turns = sem("pool_turns")
        x_in, wb_in = sem("x_in"), sem("wb_in")
        xstd, xrstd, xn_ready, xT_ps, hT_ready = sem("xstd"), sem("xrstd"), sem("xn_ready"), sem("xT_ps"), sem("hT_ready")
        z_ps, c_ps, z_ready, c_ready, cstd = sem("z_ps"), sem("c_ps"), sem("z_ready"), sem("c_ready"), sem("cstd")
        crstd, cn_ready, cTn_ps, cT_ready, qkv_ps = sem("crstd"), sem("cn_ready"), sem("cTn_ps"), sem("cT_ready"), sem("qkv_ps")
        qv_ready, k_ready, kr_ready = sem("qv_ready"), sem("k_ready"), sem("kr_ready")
        wsq, wss, wstd, wg_ready, wr_ready = sem("wsq"), sem("wss"), sem("wstd"), sem("wg_ready"), sem("wr_ready")
        qkT_ps, q_staged, kT_ready, q_stored = sem("qkT_ps"), sem("q_staged"), sem("kT_ready"), sem("q_stored")
        wf_in, fm_ps, fm_ready, y_ready = sem("wf_in"), sem("fm_ps"), sem("fm_ready"), sem("y_ready")
        uv_ps, uv_act, uv_dve, ft_ps, ft_ready = sem("uv_ps"), sem("uv_act"), sem("uv_dve"), sem("ft_ps"), sem("ft_ready")
        qs_in = [sem(f"qs_in{h}") for h in range(HEADS)]
        s_ps, nmax, p_ready, rinv, o_ps, o_ready = (sem("s_ps"), sem("nmax"), sem("p_ready"), sem("rinv"),
                                                    sem("o_ps"), sem("o_ready"))
        pT_ps = [sem(f"pT_ps{i}") for i in range(3)]
        pT_ready = [sem(f"pT_ready{i}") for i in range(3)]
        CS = CTX_TILES * HEADS
        wo_in, rd_in, xd_in = sem("wo_in"), sem("rd_in"), [sem("xd_in0"), sem("xd_in1")]
        o_staged, oT_ps, oT_ready, fx_ready, op_ps = sem("o_staged"), sem("oT_ps"), sem("oT_ready"), sem("fx_ready"), sem("op_ps")
        gx_ready, x1_ready, fstd, f0_ready, f_ready = sem("gx_ready"), sem("x1_ready"), sem("fstd"), sem("f0_ready"), sem("f_ready")
        xm_out, f_out, fT_ps, fTa, fTd, rt_ps = [sem("xm_out0"), sem("xm_out1")], [sem("f_out0"), sem("f_out1")], sem("fT_ps"), sem("fTa"), sem("fTd"), sem("rt_ps")
        rw_in, lexp, M_ready, rk_ps, dest_ready = sem("rw_in"), sem("lexp"), sem("M_ready"), sem("rk_ps"), sem("dest_ready")
        eo_ready, hot_ready, ids_ps, ids_ready = sem("eo_ready"), sem("hot_ready"), sem("ids_ps"), sem("ids_ready")
        we_in = [sem(f"we_in{u}") for u in range(3)]
        idx_ready, xg_in = sem("idx_ready"), [sem("xg_in0"), sem("xg_in1")]
        bT_ps, bTa, bTd, gu_ps, gexp, act_ready, aT_ps, aT_ready, yb_ps, yba, ybd = (
            sem("bT_ps"), sem("bTa"), sem("bTd"), sem("gu_ps"), sem("gexp"), sem("act_ready"), sem("aT_ps"),
            sem("aT_ready"), sem("yb_ps"), sem("yba"), sem("ybd"))
        yb_out = [sem("yb_out0"), sem("yb_out1")]
        g2_in, y_in, xm_in, xo_ready, xo_out = sem("g2_in"), [sem("y_in0"), sem("y_in1")], [sem("xm_in0"), sem("xm_in1")], sem("xo_ready"), [sem("xo_out0"), sem("xo_out1")]
        cmb = sem("cmb")

        block = es.enter_context(nc.Block())

        def ge(eng, s, v):
            if not isinstance(v, int) or v > 0:
                eng.wait_ge(s, v)

        class Chain:

            def __init__(self, eng, s):
                self.eng, self.s, self.n, self.base = eng, s, 0, 0

            def add(self, ins):
                ins.then_inc(self.s, 1)
                self.n += 1

            def wait(self):
                ge(self.eng, self.s, self.base + self.n)

            def __call__(self, ins):
                self.add(ins)
                self.wait()

        def loop(eng, chain, lo, hi, body):
            if chain is None:
                with eng.Fori(lo // 2, hi // 2) as j:
                    body(2 * j, j, 0)
                    body(2 * j + 1, j, 1)
                return
            b0, n0 = chain.base, chain.n
            per = count(chain, body)
            with eng.Fori(lo // 2, hi // 2) as j:
                chain.base = b0 + n0 + (j - lo // 2) * per
                chain.n = 0
                body(2 * j, j, 0)
                body(2 * j + 1, j, 1)
                assert chain.n == per, (chain.n, per)
            chain.base, chain.n = b0, n0 + (hi // 2 - lo // 2) * per

        def count(chain, body):
            return 2 * body.steps

        def mixer_steps(eng, chain, step):
            step(-1, -1, 1, cur=False, qkv=False, qt=False)
            step(0, 0, 0, qkv=False, qt=False)
            step(1, 0, 1, qt=False)
            loop(eng, chain, 2, TILES - 2, step)
            step(TILES - 2, TILES // 2 - 1, 0)
            step(TILES - 1, TILES // 2 - 1, 1, nxt=False)
            step(TILES, TILES // 2, 0, cur=False, nxt=False)
            step(TILES + 1, TILES // 2, 1, cur=False, nxt=False, qkv=False)

        def context_steps(l, attend, ahead):
            n0 = TILES * l
            tiles = [(n0 + t, CTX_TILES, t) for t in range(CTX_TILES)] if l == 0 else []
            nl = n0 + len(tiles)
            steps = [(n, h, nk, t) for n, nk, t in tiles for h in range(HEADS)]
            after = [(n, h, nk) for n, h, nk, t in steps] + [(nl, 0, TILES), (nl, 1, TILES)]
            ahead(*after[0])
            ahead(*after[1])
            for i, st in enumerate(steps):
                attend(*st, after[i + 2])
            return nl

        def lat_steps(attend, n, tile, last):
            for h in range(HEADS):
                nxt = None if last and h >= HEADS - 2 else (n + (h >= HEADS - 2), (h + 2) % HEADS, TILES)
                attend(n, h, TILES, tile, nxt)

        (xbuf, xn, hT_, c0, c1, cn, cT_, Wr, Wq, Wg, rt, qst_) = take(
            [D, D, D, CW, CW, 384, 384, 2 * HEADS * QK, 2 * HEADS * QK, 2 * HEADS * QK, 512, HEADS * P])
        csb = [c0, c1]
        hT = hT_.rearrange("p (k n) -> p k n", k=KD)
        cT = cT_.rearrange("p (k n) -> p k n", k=3)
        W4 = [w.rearrange("p (z h d) -> p z h d", z=2, h=HEADS) for w in (Wr, Wq, Wg)]
        W3 = [w.rearrange("p (h d) -> p h d", d=QK) for w in (Wr, Wq, Wg)]
        qst = qst_.rearrange("p (h n) -> p h n", h=HEADS)
        Fd, Fs, Yf = take([2048, 2048, 4096])
        QS, p0, p1, pT0, pT1 = take([HEADS * P, TOK, TOK, TOK, TOK])
        QS = QS.rearrange("p (h n) -> p h n", h=HEADS)
        pr = [p0, p1]
        pT = [a.rearrange("p (j n) -> p j n", n=P) for a in (pT0, pT1)]
        xd0, xd1, Ost, mx0, mx1, tg, ff0, ff1, fTb = take([D, D, 512, D, D, D, D, D, D])
        xd, mx = [xd0, xd1], [a.rearrange("p (k n) -> p k n", k=KD) for a in (mx0, mx1)]
        fr = [ff0, ff1]
        fT = fTb.rearrange("p (k n) -> p k n", k=KD)
        xg0, xg1, bt0, bt1, Es, Rs, a0, a1, at0, yo0, yo1 = take([D, D, D, D, DE, DE, DE, DE, DE, D, D])
        xg, bT = [xg0, xg1], [a.rearrange("p (k n) -> p k n", k=KD) for a in (bt0, bt1)]
        aa = [a0, a1]
        aT = at0.rearrange("p (k n) -> p k n", k=2)
        yo = [yo0, yo1]
        G2, ya0, ya1, yb0, yb1, xm0, xm1 = take([2 * D, D, D, D, D, D, D])
        G2 = G2.rearrange("p (s n) -> p s n", s=2)
        ya, yb, xm = [ya0, ya1], [yb0, yb1], [xm0, xm1]
        NT10 = TILES * NE
        (LG, SCO, BIA, MK, T1, T2, OH1, OH2, MM, PRE, PREb, DS) = take([NT10] * 12)
        G6v, GSv, GW, NBL, NBI_, PE1, PE2, CB, CB2, USE, ORD, ORD2 = [R2[:, 2048 + o:2048 + o + n] for o, n in
            ((0, 240), (240, 40), (280, 40), (320, 16), (336, 16), (352, 16), (368, 16), (384, 576), (960, 40), (1400, 16), (1416, 16), (1432, 16))]
        NBI = NBI_.bitcast(I32)
        SLO, SHI = R2[:, 3200:3200 + 2 * TILES], R2[:, 3232:3232 + 2 * TILES]
        SHI_ = R2[:, 3264:3264 + 2 * TILES].bitcast(I32)
        HOT = R2[:, 4096:4096 + 2 * TILES * P].rearrange("p (i n) -> p i n", n=P)
        HOTB = R2[:, 6656:6656 + 2 * TILES * NBMAX].rearrange("p (i n) -> p i n", n=NBMAX)

        def mirrored(n):
            return 3 * (min(n, 20) // 5) + max(0, min(n, 20) % 5 - 2)

        def first_tile(l):
            return 0 if l == 0 else CTX_TILES

        def nblocks(l):
            return 2 * (TILES - first_tile(l)) + NE

        @block.sync
        def _(sp):
            sp.sem_inc(we_in[1], 16)
            sp.sem_inc(we_in[2], 16)
            sp.sem_inc(q_stored, 16)
            sp.dma_start(CST[:], cst[:, :]).then_inc(cst_in, 16)
            sp.dma_start(CR[:, 0, :], c.rearrange("a (k n) -> (a k) n", k=KD)).then_inc(cin, 16)
            sp.dma_start(CR[:, 1, :], c_ctx.rearrange("(k n) -> k n", k=KD)).then_inc(cin, 16)
            for l in range(DEPTH):
                sp.dma_start(PR[0:48, l, :], b_ada[l].rearrange("(k n) -> k n", n=P)).then_inc(prm_in, 16)
                sp.dma_start(PR[48:56, l, :], norm_mix[l].rearrange("(k n) -> k n", n=P)).then_inc(prm_in, 16)
                sp.dma_start(PR[56:64, l, :], norm_ffn[l].rearrange("(k n) -> k n", n=P)).then_inc(prm_in, 16)
                sp.dma_start(PR[64:66, l, :], q_a_norm[l].rearrange("(k n) -> k n", n=P)).then_inc(prm_in, 16)
                sp.dma_start(PR[66:67, l, :], kv_a_norm[l].rearrange("(k n) -> k n", n=P)).then_inc(prm_in, 16)

            for l in range(DEPTH):
                sp.dma_start(GN[:, l, 0, :], q_norm[l:l + 1, :].to_broadcast([P, QK])).then_inc(gn_in, 16)
                sp.dma_start(GN[:, l, 1, :], k_norm[l:l + 1, :].to_broadcast([P, QK])).then_inc(gn_in, 16)
            sp.dma_start(RW[:], router_w.rearrange("(k p) e -> p k e", p=P)).then_inc(rw_in, 16)
            sp.dma_start(RB[:], router_bias.rearrange("(a e) -> a e", a=1).to_broadcast([P, NE])).then_inc(rw_in, 16)
            def mixer_weights(l):
                sp.dma_start(WF[:].rearrange("p (g d) -> p g d", g=FG), w_fourier[l].rearrange("g c d -> c g d")).then_inc(wf_in, 16)
                sp.dma_start(win, w_in[l].rearrange("(k p) n -> p k n", p=P)).then_inc(wb_in, 16)
                sp.dma_start(wqb, w_q_b[l].rearrange("(k p) n -> p k n", p=P)).then_inc(wb_in, 16)
                sp.dma_start(wkv, w_kv_b[l]).then_inc(wb_in, 16)

            for l in range(DEPTH):
                B = TILES * l
                t0 = first_tile(l)
                if l == 0:
                    mixer_weights(0)
                for u in range(3):
                    sp.wait_ge(arow_out[u], 16 * (ADP // 3) * (l + 1))
                if l > 0:
                    sp.wait_ge(rows_out, 16)
                sp.dma_start(ROWS[:], rows_d[l].rearrange("s (j n) -> (s j) n", n=P)).then_inc(raw_in, 16)
                sp.wait_ge(rows_ready, l + 1)
                sp.dma_start(rows_d[l].rearrange("s (j n) -> (s j) n", n=P), ROWS[:]).then_inc(rows_out, 16)
                if l > 0:
                    sp.wait_ge(xo_out[0], 16 * TILES // 2)
                    sp.wait_ge(xo_out[1], 16 * TILES // 2)

                def step(t, h, u, cur=True, nxt=True, qkv=True, qt=True, l=l, B=B):
                    if nxt:
                        ge(sp, xn_ready, B + t + 1)
                        if l > 0:
                            src = xnext_d[bass.ds((t + 1) * P, P), :]
                        elif isinstance(t, int) and t + 1 < CTX_TILES:
                            src = ctx[0, (t + 1) * P:(t + 2) * P, :]
                        else:
                            src = x[0, bass.ds((t + 1 - CTX_TILES) * P, P), :]
                        sp.dma_start(xbuf, src).then_inc(x_in, 16)
                    if qt:
                        sp.wait_ge(q_staged, B + t - 1)
                        sp.dma_start(qT_d[bass.ds(t - 2, 1)].rearrange("a d n -> (a d) n"), qst_[0:QK, :]).then_inc(q_stored, 16)
                mixer_steps(sp, None, step)
                sp.wait_ge(q_stored, 16 * (B + TILES) + 16)

                QB = 0 if l == 0 else TILES

                def qload(n, tile, h):
                    if not isinstance(n, int) or n > QB:
                        sp.wait_ge(s_ps, HEADS * (n - 1) + h + 1)
                    sp.dma_start(QS[0:QK, h, :], qT_d[bass.ds(tile, 1), :, h * P:(h + 1) * P].rearrange("a d n -> (a d) n")
                                 ).then_inc(qs_in[h], 16)
                sp.wait_ge(y_ready, 2 if l == 0 else 3)
                sp.wait_ge(uv_ps, 28 if l == 0 else 48)
                n0 = QB
                if l == 0:
                    for t in range(CTX_TILES):
                        for h in range(HEADS):
                            qload(n0 + t, t, h)
                    n0 += CTX_TILES
                for h in range(HEADS):
                    qload(n0, CTX_TILES, h)
                sp.wait_ge(ft_ps, (12 if l == 0 else 20))
                sp.dma_start(wout, w_out[l].rearrange("(k p) n -> p k n", p=P)).then_inc(wo_in, 16)
                with sp.Fori(1, LAT_TILES) as j:
                    for h in range(HEADS):
                        qload(j + n0, j + CTX_TILES, h)

                sp.wait_ge(rows_out, 16 * (l + 1))
                nq = n0 + LAT_TILES
                sp.wait_ge(o_ps, HEADS * nq)
                sp.wait_ge(o_ready, HEADS * nq)
                for s in range(2):
                    sp.dma_start(rowsD[:, s].rearrange("p v n -> p (v n)"),
                                 rows_d[l, s:s + 1, 2 * D:5 * D].to_broadcast([P, 3 * D])).then_inc(rd_in, 16)

                def expert_at(o):
                    return sp.value_load(EO[0:1, bass.ds(o, 1)], min_val=0, max_val=NE - 1)

                def load_expert(e, u, l=l):
                    w = wslot[u]
                    gu = w[:, 0:KD * 2 * DE].rearrange("p (k z n) -> p k z n", k=KD, z=2)
                    for z, src in ((0, w_gate), (1, w_up)):
                        sp.dma_start(gu[:, :, z, :], src[l, bass.ds(e, 1)].rearrange("a (k p) n -> p (a k) n", p=P)
                                     ).then_inc(we_in[u], 16)
                    sp.dma_start(w[:, KD * 2 * DE:].rearrange("p (k n) -> p k n", n=D),
                                 w_down[l, bass.ds(e, 1)].rearrange("a (k p) n -> p (a k) n", p=P)).then_inc(we_in[u], 16)

                DB = 0 if l == 0 else TILES

                def dstep(t, h, u, l=l, DB=DB, t0=t0):
                    d = t + (DB - t0)
                    hh = h + (DB - t0) // 2
                    ge(sp, xm_out[u], 16 * hh)
                    if l > 0:
                        src = xnext_d[bass.ds(t * P, P), :]
                    elif isinstance(t, int) and t < CTX_TILES:
                        src = ctx[0, t * P:(t + 1) * P, :]
                    else:
                        src = x[0, bass.ds((t - CTX_TILES) * P, P), :]
                    sp.dma_start(xd[u], src).then_inc(xd_in[u], 16)

                def dstore(t, h, u, DB=DB, t0=t0):
                    d = t + (DB - t0)
                    sp.wait_ge(x1_ready, d + 1)
                    sp.dma_start(xmid_d[bass.ds(t * P, P), :], xd[u]).then_inc(xm_out[u], 16)
                    sp.wait_ge(f_ready, d + 1)
                    sp.dma_start(f_d[bass.ds(t * P, P), :], fr[u]).then_inc(f_out[u], 16)

                def dboth(t, h, u):
                    dstore(t, h, u)
                    dstep(t + 2, h + 1, u)
                dstep(t0, t0 // 2, 0)
                dstep(t0 + 1, t0 // 2, 1)
                if l == 0:
                    dboth(0, 0, 0)
                    dboth(1, 0, 1)
                loop(sp, None, CTX_TILES, TILES - 2, dboth)
                dstore(TILES - 2, TILES // 2 - 1, 0)
                dstore(TILES - 1, TILES // 2 - 1, 1)
                dn = DB + TILES - t0
                NB = nblocks(l)
                BB = 0 if l == 0 else nblocks(0)
                sp.wait_ge(eo_ready, l + 1)
                for u in range(3):
                    load_expert(expert_at(u), u)

                def expert(e, u, BB=BB):
                    fb = sp.value_load(FB[0:1, bass.ds(e - 2, 1)], min_val=0, max_val=NBMAX)
                    real = expert_at(e)
                    sp.wait_ge(yb_ps, fb + BB)
                    load_expert(real, u)
                with sp.Fori(1, NE // 3) as j:
                    for u in range(3):
                        expert(3 * j + u, u)
                expert(NE - 1, (NE - 1) % 3)
                if l == 0:
                    mixer_weights(1)

                sp.wait_ge(yb_ps, BB + NB)
                sp.wait_ge(yb_out[0], 16 * (BB + NB) // 2)
                sp.wait_ge(yb_out[1], 16 * (BB + NB) // 2)
                for s in range(2):
                    sp.dma_start(G2[:, s], rows_d[l, s:s + 1, 5 * D:6 * D].to_broadcast([P, D])).then_inc(g2_in, 16)

                def cload(t, h, u, DB=DB, t0=t0):
                    hh = h + (DB - t0) // 2
                    ge(sp, xo_out[u], 16 * hh)
                    sp.dma_start(xm[u], xmid_d[bass.ds(t * P, P), :]).then_inc(xm_in[u], 16)

                def cstore(t, h, u, DB=DB, t0=t0, l=l):
                    sp.wait_ge(xo_ready, t + (DB - t0) + 1)
                    dst = xnext_d[bass.ds(t * P, P), :] if l == 0 else out[0, bass.ds((t - CTX_TILES) * P, P), :]
                    sp.dma_start(dst, xm[u]).then_inc(xo_out[u], 16)

                def cboth(t, h, u):
                    cstore(t, h, u)
                    cload(t + 2, h + 1, u)
                cload(t0, t0 // 2, 0)
                cload(t0 + 1, t0 // 2, 1)
                loop(sp, None, t0, TILES - 2, cboth)
                cstore(TILES - 2, TILES // 2 - 1, 0)
                cstore(TILES - 1, TILES // 2 - 1, 1)
            dn = TILES + LAT_TILES
            for u in range(2):
                sp.wait_ge(xo_out[u], 16 * dn // 2)
                sp.wait_ge(xm_out[u], 16 * dn // 2)

        @block.tensor
        def _(pe):
            pe.wait_ge(cst_in, 16)
            pe.wait_ge(prm_in, 16 * 5 * DEPTH)
            pe.wait_ge(csilu, 1)
            for s in range(2):
                mm = pe.transpose(bank(7, 8 * s, 8 * s + 8), CR[:, s, :], ident[0:KD, 0:KD])
            mm.then_inc(cT_ps, 1)
            for l in range(DEPTH):
                mm = pe.transpose(bank(6, P * l, P * l + 67), PR[:, l, :], ident[0:67, 0:67])
            mm.then_inc(prm_ps, 1)
            pe.wait_ge(sc_ready, 1)

            for l in range(DEPTH):
                B = TILES * l
                t0 = first_tile(l)
                if l > 0:
                    pe.wait_ge(yba, nblocks(0))
                    pe.wait_ge(ybd, nblocks(0))

                def ada(j, l=l):
                    for u in range(3):
                        pe.wait_ge(ada_in[u], 16 * (j + (ADP // 3 * l + 1)))
                        ge(pe, arow_ready, 3 * j + (ADP * l + u - 2))
                        for kk in range(KD):
                            mm = pe.matmul(PS[0:2, u, :], SC[:, kk, :], wada[u][:, kk, :], start=(kk == 0), stop=(kk == KD - 1))
                        mm.then_inc(ada_mm, 1)
                ada(0)
                with pe.Fori(1, ADP // 3) as j:
                    ada(j)
                pe.wait_ge(raw_in, 16 * (l + 1))
                pe.transpose(PS[:, 3, 0:96], ROWS[:], ident[0:96, 0:96]).then_inc(raw_ps, 1)
                pe.wait_ge(mod_done, l + 1)
                pe.transpose(PS[0:96, 4, 0:P], MOD[:, l].rearrange("p s j -> p (s j)"), ident).then_inc(rows_ps, 1)
                pe.wait_ge(wf_in, 16 * (l + 1))
                pe.matmul(bank(6), k("cc"), WF[:], start=True, stop=True)
                pe.matmul(bank(7), k("nsc"), WF[:], start=True, stop=True).then_inc(fm_ps, 1)
                pe.wait_ge(fm_ready, l + 1)
                pe.wait_ge(wb_in, 48 * (l + 1))
                pe.wait_ge(rows_ready, l + 1)

                def step(t, h, u, cur=True, nxt=True, qkv=True, qt=True, B=B):
                    if cur:
                        pe.wait_ge(hT_ready, B + t + 1)
                        ge(pe, z_ready, B + t)
                        for kk in range(KD):
                            mm = pe.matmul(bank(3), hT[:, kk, :], win[:, kk, CW:INW], start=(kk == 0), stop=(kk == KD - 1))
                        mm.then_inc(z_ps, 1)
                        ge(pe, cstd, B + t)
                        for kk in range(KD):
                            mm = pe.matmul(bank(2, 0, CW), hT[:, kk, :], win[:, kk, 0:CW], start=(kk == 0), stop=(kk == KD - 1))
                        mm.then_inc(c_ps, 1)
                    if qt:
                        pe.wait_ge(wr_ready, B + t - 1)
                        for hh in range(2 * HEADS):
                            mm = pe.transpose(PS[0:QK, 4 + hh // 4, (hh % 4) * P:(hh % 4 + 1) * P], W3[2][:, hh, :], ident)
                        mm.then_inc(qkT_ps, 1)
                    if nxt:
                        pe.wait_ge(xn_ready, B + t + 2)
                        for kk in range(KD):
                            mm = pe.transpose(bank(kk // 4, (kk % 4) * P, (kk % 4 + 1) * P), xn[:, kk * P:(kk + 1) * P], ident)
                        mm.then_inc(xT_ps, 1)
                    if qkv:
                        pe.wait_ge(cT_ready, B + t)
                        if qt:
                            pe.wait_ge(q_staged, B + t - 1)
                            pe.wait_ge(kT_ready, B + t - 1)
                        for kk in range(2):
                            pe.matmul(bank(4, 0, 480), cT[:, kk, :], wqb[:, kk, 0:480], start=(kk == 0), stop=(kk == 1))
                        for kk in range(2):
                            pe.matmul(bank(5, 0, 288), cT[:, kk, :], wqb[:, kk, 480:768], start=(kk == 0), stop=(kk == 1))
                        pe.matmul(bank(6), cT[:, 2, :], wkv[:, 0:512], start=True, stop=True)
                        pe.matmul(bank(7), cT[:, 2, :], wkv[:, 512:1024], start=True, stop=True).then_inc(qkv_ps, 1)
                    if cur:
                        pe.wait_ge(cn_ready, B + t + 1)
                        if qkv:
                            pe.wait_ge(qv_ready, B + t)
                        for kk in range(3):
                            mm = pe.transpose(bank(5, kk * P, (kk + 1) * P), cn[:, kk * P:(kk + 1) * P], ident)
                        mm.then_inc(cTn_ps, 1)
                mixer_steps(pe, None, step)

                pe.wait_ge(y_ready, 1 if l == 0 else 3)
                pe.wait_ge(q_staged, B + TILES)
                pe.wait_ge(kT_ready, B + TILES)
                ub = 28 * l
                RES = [(0, (0,)), (4, (1,)), (2, (2, 3)), (1, (4, 5)), (3, (6, 7))]
                n = 0
                for g in range(FG):
                    for r, parts in RES:
                        if n >= 4:
                            pe.wait_ge(uv_act, 28 * l + n - 3)
                            ge(pe, uv_dve, 12 * l + mirrored(n - 3))
                        for i, part in enumerate(parts):
                            lhs = Yf[:, part * FW + g * FD:part * FW + (g + 1) * FD]
                            mm = pe.matmul(bank(n % 4, 0, 256), lhs, k("tw", r * 384 + (0 if i else P), r * 384 + (256 if i else 384)),
                                           start=(i == 0), stop=(i == len(parts) - 1))
                        mm.then_inc(uv_ps, 1)
                        n += 1
                pe.wait_ge(uv_act, 28 * l + 20)
                ge(pe, uv_dve, 12 * l + mirrored(20))
                m = 0
                for g in range(FG):
                    for ch in range(2):
                        if m >= 4:
                            pe.wait_ge(ft_ready, (12 * l) + m - 3)
                        for z in range(2):
                            mm = pe.matmul(bank(4 + m % 4), FM[:, z, g * FD:(g + 1) * FD], UV[:, z, g, ch * 512:(ch + 1) * 512],
                                           start=(z == 0), stop=(z == 1))
                        mm.then_inc(ft_ps, 1)
                        m += 1
                if l == 0:
                    pe.wait_ge(y_ready, 2)
                    for g in range(FG):
                        for i, r in enumerate((0, 4)):
                            pe.wait_ge(uv_act, 28 * l + n - 3)
                            ge(pe, uv_dve, 12 * l + mirrored(n - 3))
                            pe.matmul(bank(n % 4, 0, 256), Fd[:, i * FW + g * FD:i * FW + (g + 1) * FD],
                                      k("tw", r * 384 + P, r * 384 + 384), start=True, stop=True).then_inc(uv_ps, 1)
                            n += 1
                    pe.wait_ge(uv_act, 28 * l + 28)
                    ge(pe, uv_dve, 12 * l + mirrored(28))
                    for g in range(FG):
                        pe.wait_ge(ft_ready, m - 3)
                        for z in range(2):
                            mm = pe.matmul(bank(4 + m % 4, 0, CTX), FM[:, z, g * FD:(g + 1) * FD], UV[:, z, g, 0:CTX],
                                           start=(z == 0), stop=(z == 1))
                        mm.then_inc(ft_ps, 1)
                        m += 1
                pe.wait_ge(ft_ready, 12 if l == 0 else 20)

                def scores(n, h, nk, parts=(0, 1, 2)):
                    b = 3 * (h % 2)
                    if 0 in parts:
                        pe.wait_ge(qs_in[h], 16 * (n + 1))
                    for i in parts:
                        w = min(512, nk * P - 512 * i)
                        if w > 0:
                            mm = pe.matmul(bank(b + i, 0, w), QS[0:QK, h, :], kT[0:QK, h, 512 * i:512 * i + w], start=True, stop=True)
                            if 512 * i + w == nk * P:
                                mm.then_inc(s_ps, 1)

                def transposes(h, nk, ci):
                    for j in range(4 * ci, min(4 * ci + 4, nk)):
                        mm = pe.transpose(bank(6 + ci % 2, (j - 4 * ci) * P, (j - 4 * ci + 1) * P), pr[h % 2][:, j * P:(j + 1) * P], ident)
                    mm.then_inc(pT_ps[ci], 1)

                def attend(n, h, nk, tile, nxt):
                    s = HEADS * n + h
                    pe.wait_ge(p_ready, s + 1)
                    transposes(h, nk, 0)
                    ge(pe, o_ready, s)
                    if nk > 4:
                        transposes(h, nk, 1)
                    if nxt:
                        scores(*nxt, parts=(0,))
                    if nk > 4:
                        pe.wait_ge(pT_ready[0], s + 1)
                        transposes(h, nk, 2)
                    if nxt:
                        scores(*nxt, parts=(1, 2))
                    for ci in range(-(-nk // 4)):
                        pe.wait_ge(pT_ready[ci], s + 1 - (CS if ci else 0))
                    for j in range(nk):
                        mm = pe.matmul(bank(7, 0, VDIM), pT[h % 2][:, j, :], V[:, j * 512 + h * VDIM:j * 512 + (h + 1) * VDIM],
                                       start=(j == 0), stop=(j == nk - 1))
                    mm.then_inc(o_ps, 1)

                n0 = context_steps(l, attend, scores)
                with pe.Fori(0, LAT_TILES - 1) as j:
                    lat_steps(attend, j + n0, j + CTX_TILES, False)
                lat_steps(attend, n0 + LAT_TILES - 1, TILES - 1, True)

                nq = n0 + LAT_TILES
                DB = 0 if l == 0 else TILES
                pe.wait_ge(o_ready, HEADS * nq)
                pe.wait_ge(wo_in, 16 * (l + 1))
                pe.wait_ge(rw_in, 32)

                def otrans(t, u, DB=DB, t0=t0):
                    d = t + (DB - t0)
                    pe.wait_ge(o_staged, d + 1)
                    ge(pe, oT_ready, d)
                    for kk in range(4):
                        mm = pe.transpose(bank(4, kk * P, (kk + 1) * P), Ost[:, kk * P:(kk + 1) * P], ident)
                    mm.then_inc(oT_ps, 1)

                def project(t, u, DB=DB, t0=t0):
                    d = t + (DB - t0)
                    pe.wait_ge(oT_ready, d + 1)
                    pe.wait_ge(fx_ready, d + 1)
                    ge(pe, gx_ready, d - 1)
                    for half in range(2):
                        for kk in range(KD):
                            mm = pe.matmul(bank(2 * u + half), mx[u][:, kk, :], wout[:, kk, half * 512:(half + 1) * 512],
                                           start=(kk == 0), stop=(kk == KD - 1))
                    mm.then_inc(op_ps, 1)

                def route(t, u, DB=DB, t0=t0):
                    d = t + (DB - t0)
                    pe.wait_ge(f_ready, d + 1)
                    ge(pe, fTa, d)
                    ge(pe, fTd, d)
                    for kk in range(KD):
                        mm = pe.transpose(bank(5 + kk // 4, (kk % 4) * P, (kk % 4 + 1) * P), fr[u][:, kk * P:(kk + 1) * P], ident)
                    mm.then_inc(fT_ps, 1)
                    pe.wait_ge(fTa, d + 1)
                    pe.wait_ge(fTd, d + 1)
                    for kk in range(KD):
                        mm = pe.matmul(PS[:, 7, bass.ds(t * NE, NE)], fT[:, kk, :], RW[:, kk, :], start=(kk == 0), stop=(kk == KD - 1))
                    mm.then_inc(rt_ps, 1)

                def dstep(t, h, u, first=False, last=False):
                    project(t, u)
                    if not last:
                        otrans(t + 1, 1 - u)
                    if not first:
                        route(t - 1, 1 - u)
                otrans(t0, 0)
                dstep(t0, t0 // 2, 0, first=True)
                dstep(t0 + 1, t0 // 2, 1)
                loop(pe, None, t0 + 2, TILES - 2, dstep)
                dstep(TILES - 2, 0, 0)
                dstep(TILES - 1, 0, 1, last=True)
                route(TILES - 1, 1)

                NT = (TILES - t0) * NE
                pe.wait_ge(M_ready, l + 1)
                pe.matmul(bank(0, 0, NT), k("tri"), MM[:, 0:NT], start=True, stop=True)
                pe.matmul(bank(1, 0, NT), k("ones"), MM[:, 0:NT], start=True, stop=True).then_inc(rk_ps, 1)
                NB = nblocks(l)
                for i in range(2 * (TILES - t0)):
                    pe.wait_ge(hot_ready, 2 * TILES * l + i + 1)
                    mm = pe.matmul(bank(2, 0, NB), HOT[:, i, :], HOTB[:, i, 0:NB], start=(i == 0), stop=(i == 2 * (TILES - t0) - 1))
                mm.then_inc(ids_ps, 1)
                pe.wait_ge(ids_ready, l + 1)

                BB = 0 if l == 0 else nblocks(0)

                def btrans(b, h, u, BB=BB):
                    pe.wait_ge(xg_in[u], 16 * (h + BB // 2 + 1))
                    ge(pe, bTa, BB + b)
                    ge(pe, bTd, BB + b)
                    for kk in range(KD):
                        mm = pe.transpose(bank(kk // 4, (kk % 4) * P, (kk % 4 + 1) * P), xg[u][:, kk * P:(kk + 1) * P], ident)
                    mm.then_inc(bT_ps, 1)

                def gate_up(b, e, u, BB=BB, l=l):
                    pe.wait_ge(we_in[0], (e // 3) * 48 + 48 * (6 * l + 1))
                    pe.wait_ge(we_in[1], ((e + 2) // 3) * 48 + 48 * 5 * l + 16)
                    pe.wait_ge(we_in[2], ((e + 1) // 3) * 48 + 48 * 5 * l + 16)
                    pe.wait_ge(bTa, BB + b + 1)
                    pe.wait_ge(bTd, BB + b + 1)
                    ge(pe, act_ready, BB + b - 1)
                    off = (e % 3) * WSLOT
                    for kk in range(KD):
                        mm = pe.matmul(bank(2 + u), bT[u][:, kk, :], KV[:, bass.ds(off + kk * 512, 512)],
                                       start=(kk == 0), stop=(kk == KD - 1))
                    mm.then_inc(gu_ps, 1)

                def down(b, e, u, BB=BB):
                    pe.wait_ge(act_ready, BB + b + 1)
                    ge(pe, aT_ready, BB + b)
                    for kk in range(2):
                        mm = pe.transpose(bank(4, kk * P, (kk + 1) * P), aa[u][:, kk * P:(kk + 1) * P], ident)
                    mm.then_inc(aT_ps, 1)
                    pe.wait_ge(aT_ready, BB + b + 1)
                    ge(pe, yba, BB + b)
                    ge(pe, ybd, BB + b)
                    off = (e % 3) * WSLOT + KD * 2 * DE
                    for half in range(2):
                        for kk in range(2):
                            mm = pe.matmul(bank(5 + half), aT[:, kk, :], KV[:, bass.ds(off + kk * D + half * 512, 512)],
                                           start=(kk == 0), stop=(kk == 1))
                    mm.then_inc(yb_ps, 1)

                def expert_of(b):
                    return pe.value_load(BE[0:1, bass.ds(b, 1)], min_val=0, max_val=NE - 1)

                btrans(0, 0, 0)
                gate_up(0, expert_of(0), 0)
                btrans(1, 0, 1)
                def pair(j):
                    e0, e1, e2 = expert_of(2 * j), expert_of(2 * j + 1), expert_of(2 * j + 2)
                    gate_up(2 * j + 1, e1, 1)
                    btrans(2 * j + 2, j + 1, 0)
                    down(2 * j, e0, 0)
                    gate_up(2 * j + 2, e2, 0)
                    btrans(2 * j + 3, j + 1, 1)
                    down(2 * j + 1, e1, 1)
                pair(0)
                with pe.Fori(1, NB // 2 - 1) as j:
                    pair(j)
                e0, e1 = expert_of(NB - 2), expert_of(NB - 1)
                gate_up(NB - 1, e1, 1)
                down(NB - 2, e0, 0)
                down(NB - 1, e1, 1)

        @block.scalar
        def _(act):
            def ada_load(l, t, u):
                act.dma_start(wada[u], w_ada[l].rearrange("(k p) n -> p k n", p=P)[:, :, bass.ds(t * 512, 512)]).then_inc(ada_in[u], 16)

            act.wait_ge(cin, 32)
            for u in range(3):
                ada_load(0, u, u)
            act.wait_ge(dst_, 1)
            act.wait_ge(cin, 32)
            act.activation(CE[:], CR[:], ACT.Exp, scale=-1.0).then_inc(cexp, 1)
            for l in range(DEPTH):
                B = TILES * l
                t0 = first_tile(l)
                ch = Chain(act, ast_) if l == 0 else ch
                if l > 0:
                    act.wait_ge(yb_ps, nblocks(0))
                    for u in range(3):
                        ada_load(l, u, u)

                def ada(j, ahead, l=l):
                    for u in range(3):
                        act.wait_ge(ada_mm, 3 * j + (ADP * l + u + 1))
                        if ahead:
                            ada_load(l, 3 * j + (u + 3), u)
                        ge(act, arow_out[u], 16 * (j + ADP // 3 * l))
                        act.activation(arow[u], PS[0:2, u, :], ACT.Copy).then_inc(arow_ready, 1)
                        act.wait_ge(arow_ready, 3 * j + (ADP * l + u + 1))
                        act.dma_start(rows_d[l, :, bass.ds((3 * j + u) * 512, 512)], arow[u]).then_inc(arow_out[u], 16)
                ada(0, True)
                with act.Fori(1, ADP // 3 - 1) as j:
                    ada(j, True)
                ada(ADP // 3 - 1, False)

                def step(t, h, u, cur=True, nxt=True, qkv=True, qt=True, B=B, l=l):
                    if nxt:
                        act.wait_ge(x_in, 16 * (B + t + 2))
                        ge(act, wss, B + t - 1)
                        ge(act, xrstd, B + t + 1)
                        act.activation(Wq[:, 0:D], xbuf, ACT.Square, scale=1.0 / 32, accum_out=sm[:, 0:1]).then_inc(ast_, 1)
                        nch = ch.n
                        ch.n += 1
                        ch.wait()
                        act.activation(sm[:, 1:2], sm[:, 0:1], ACT.Sqrt, bias=EPSC[:, 0:1]).then_inc(xstd, 1)
                    if cur:
                        act.wait_ge(z_ps, B + t + 1)
                        act.activation(ZO[:, bass.ds(t * FW, FW)], bank(3), ACT.Copy).then_inc(z_ready, 1)
                        act.wait_ge(c_ps, B + t + 1)
                        ge(act, kr_ready, B + t - 1)
                        ge(act, crstd, B + t)
                        act.activation(csb[u], bank(2, 0, CW), ACT.Copy).then_inc(c_ready, 1)
                        act.activation(Wq[:, 0:QR], bank(2, 0, QR), ACT.Square, scale=1.0 / 16, accum_out=sm[:, 4:5])
                        act.activation(Wq[:, QR:QR + KVR], bank(2, QR, QR + KVR), ACT.Square, scale=float(KVR) ** -0.5,
                                       accum_out=sm[:, 5:6]).then_inc(ast_, 1)
                        ch.n += 1
                        ch.wait()
                        act.activation(sm[:, 6:8], sm[:, 4:6], ACT.Sqrt, bias=EPSC[:, 0:1]).then_inc(cstd, 1)
                    if qt:
                        act.wait_ge(qkT_ps, B + t - 1)
                        ge(act, q_stored, 16 * (B + t - 2) + 16)
                        act.activation(qst[0:QK, 0:4, :].rearrange("p h n -> p (h n)"), PS[0:QK, 4, :], ACT.Copy)
                        act.activation(qst[0:QK, 4:8, :].rearrange("p h n -> p (h n)"), PS[0:QK, 5, :], ACT.Copy).then_inc(q_staged, 1)
                    if qkv:
                        act.wait_ge(qkv_ps, B + t)
                        ge(act, wg_ready, B + t - 1)
                        act.activation(Wr[:, 0:480], bank(4, 0, 480), ACT.Copy).then_inc(ast_, 1)
                        act.activation(Wr[:, 480:768], bank(5, 0, 288), ACT.Copy).then_inc(ast_, 1)
                        act.wait_ge(k_ready, B + t)
                        for i in range(2):
                            ins = act.activation(V[:, bass.ds((t - 1) * 512 + i * 256, 256)].rearrange("p (h d) -> p h d", h=4),
                                                 bank(6 + i).rearrange("p (h d) -> p h d", h=4)[:, :, NOPE:], ACT.Copy)
                        ins.then_inc(qv_ready, 1)
                        ch.n += 2
                        ch.wait()
                        act.wait_ge(k_ready, B + t)
                        act.wait_ge(kr_ready, B + t)
                        act.activation(Wq, Wr, ACT.Square, scale=float(QK) ** -0.5).then_inc(wsq, 1)
                        act.wait_ge(wss, B + t)
                        act.activation(sm[:, 32:48], sm[:, 16:32], ACT.Sqrt, bias=EPSC[:, 0:1]).then_inc(wstd, 1)
                step.steps = 4
                mixer_steps(act, ch, step)

                n = 0
                for g in range(FG):
                    for r in (0, 4, 2, 1, 3):
                        act.wait_ge(uv_ps, 28 * l + n + 1)
                        act.activation(UV[:, :, g, r:SEQ:8], bank(n % 4, 0, 256).rearrange("p (z m) -> p z m", z=2),
                                       ACT.Copy).then_inc(uv_act, 1)
                        n += 1
                for m in range(8):
                    g, chk = m // 2, m % 2
                    if m % 2 == 0:
                        continue
                    act.wait_ge(ft_ps, 12 * l + m + 1)
                    act.wait_ge(ft_ready, 12 * l + m)
                    act.activation(FT[:, g, CTX + chk * 512:CTX + (chk + 1) * 512], bank(4 + m % 4), ACT.Copy).then_inc(ft_ready, 1)
                if l == 0:
                    for g in range(FG):
                        for i in range(2):
                            act.wait_ge(uv_ps, n + 1)
                            act.wait_ge(ft_ps, 8)
                            act.activation(UV[:, :, g, i:CTX:2], bank(n % 4, 0, 256).rearrange("p (z m) -> p z m", z=2),
                                           ACT.Copy, scale=2.0).then_inc(uv_act, 1)
                            n += 1

                def soft(n, h, nk):
                    s = HEADS * n + h
                    b = 3 * (h % 2)
                    act.wait_ge(nmax, s + 1)
                    act.activation(pr[h % 2][:, 0:nk * P], PS[:, b:b + 3, :].rearrange("p b n -> p (b n)")[:, 0:nk * P], ACT.Exp,
                                   bias=sm[:, 50 + h % 2:51 + h % 2], scale=SCALE, accum_out=sm[:, 52 + h % 2:53 + h % 2]
                                   ).then_inc(p_ready, 1)

                def attend(n, h, nk, tile, nxt):
                    s = HEADS * n + h
                    if nk > 4:
                        act.wait_ge(pT_ps[1], s + 1 - CS)
                        act.activation(pT[h % 2][:, 4:8, :].rearrange("p j n -> p (j n)"), bank(7), ACT.Copy).then_inc(pT_ready[1], 1)
                    act.wait_ge(rinv, s + 1)
                    act.wait_ge(o_ps, s + 1)
                    act.activation(ZO[:, bass.ds(tile * 512 + h * VDIM, VDIM)], bank(7, 0, VDIM), ACT.Copy,
                                   scale=sm[:, 54 + h % 2:55 + h % 2]).then_inc(o_ready, 1)
                    if nxt:
                        soft(*nxt)

                n0 = context_steps(l, attend, soft)
                with act.Fori(0, LAT_TILES - 1) as j:
                    lat_steps(attend, j + n0, j + CTX_TILES, False)
                lat_steps(attend, n0 + LAT_TILES - 1, TILES - 1, True)

                DB = 0 if l == 0 else TILES

                def oev(t, u, DB=DB, t0=t0):
                    d = t + (DB - t0)
                    act.wait_ge(oT_ps, d + 1)
                    ge(act, op_ps, d - 1)
                    act.activation(mx[u][:, 0:4, :].rearrange("p k n -> p (k n)"), bank(4), ACT.Copy).then_inc(oT_ready, 1)

                def frms(t, u, DB=DB, t0=t0):
                    d = t + (DB - t0)
                    act.wait_ge(x1_ready, d + 1)
                    ge(act, f0_ready, d)
                    act.activation(tg, xd[u], ACT.Square, scale=1.0 / 32, accum_out=sm[:, 0:1]).then_inc(ast_, 1)
                    ch.n += 1
                    ch.wait()
                    act.activation(sm[:, 1:2], sm[:, 0:1], ACT.Sqrt, bias=EPSC[:, 0:1]).then_inc(fstd, 1)

                def fTev(t, u, DB=DB, t0=t0):
                    d = t + (DB - t0)
                    act.wait_ge(fT_ps, d + 1)
                    ge(act, rt_ps, d)
                    act.activation(fT[:, 0:4, :].rearrange("p k n -> p (k n)"), bank(5), ACT.Copy).then_inc(fTa, 1)

                def dstep(t, h, u, first=False, last=False):
                    if not last:
                        oev(t + 1, 1 - u)
                    frms(t, u) if first or True else None
                    if not first:
                        pass

                def dact(t, h, u, first=False, last=False):
                    if not last:
                        oev(t + 1, 1 - u)
                    if not first:
                        fTev(t - 1, 1 - u)
                    frms(t, u)
                dact.steps = 1
                oev(t0, 0)
                dact(t0, 0, 0, first=True)
                dact(t0 + 1, 0, 1)
                loop(act, ch, t0 + 2, TILES - 2, dact)
                dact(TILES - 2, 0, 0)
                dact(TILES - 1, 0, 1, last=True)
                fTev(TILES - 1, 1)

                NT = (TILES - t0) * NE
                DN = DB + TILES - t0
                act.wait_ge(rt_ps, DN)
                for u in range(2):
                    act.wait_ge(xm_out[u], 16 * DN // 2)
                    act.wait_ge(f_out[u], 16 * DN // 2)
                act.activation(LG[:, 0:NT], bank(7, t0 * NE, TILES * NE), ACT.Exp, scale=-1.0).then_inc(lexp, 1)

                BB = 0 if l == 0 else nblocks(0)
                NB = nblocks(l)
                act.wait_ge(ids_ready, l + 1)

                def bev(b, u, BB=BB):
                    act.wait_ge(bT_ps, BB + b + 1)
                    ge(act, gu_ps, BB + b - 1)
                    act.activation(bT[u][:, 0:4, :].rearrange("p k n -> p (k n)"), bank(0), ACT.Copy).then_inc(bTa, 1)

                def gev(b, u, BB=BB):
                    act.wait_ge(gu_ps, BB + b + 1)
                    ge(act, act_ready, BB + b)
                    act.activation(Es, bank(2 + u, 0, DE), ACT.Exp, scale=-1.0).then_inc(gexp, 1)

                def yev(b, h, u, BB=BB):
                    act.wait_ge(yb_ps, BB + b + 1)
                    ge(act, yb_out[u], 16 * (h + BB // 2))
                    act.activation(yo[u][:, 0:512], bank(5), ACT.Copy).then_inc(yba, 1)
                    act.wait_ge(yba, BB + b + 1)
                    act.wait_ge(ybd, BB + b + 1)
                    act.dma_start(yb_d[bass.ds(b * P, P), :], yo[u]).then_inc(yb_out[u], 16)
                bev(0, 0)
                gev(0, 0)
                bev(1, 1)
                def pair(j):
                    gev(2 * j + 1, 1)
                    bev(2 * j + 2, 0)
                    yev(2 * j, j, 0)
                    gev(2 * j + 2, 0)
                    bev(2 * j + 3, 1)
                    yev(2 * j + 1, j, 1)
                pair(0)
                with act.Fori(1, NB // 2 - 1) as j:
                    pair(j)
                gev(NB - 1, 1)
                yev(NB - 2, NB // 2 - 1, 0)
                yev(NB - 1, NB // 2 - 1, 1)

        @block.gpsimd
        def _(pool):
            def carry():
                pool.sem_inc(pool_turns, 1)

            pc = Chain(pool, pst_)
            for l in range(DEPTH):
                B = TILES * l
                t0 = first_tile(l)
                if l == 0:
                    pool.wait_ge(gn_in, 16 * 2 * DEPTH)

                def step(t, h, u, cur=True, nxt=True, qkv=True, qt=True, B=B, l=l):
                    if nxt:
                        pool.wait_ge(xrstd, B + t + 2)
                        ge(pool, xT_ps, B + t + 1)
                        pool.wait_ge(x_in, 16 * (B + t + 2))
                        carry()
                        pool.tensor_scalar(xn, xbuf, sm[:, 2:3], None, ALU.mult).then_inc(xn_ready, 1)
                    if cur:
                        pool.wait_ge(crstd, B + t + 1)
                        ge(pool, cTn_ps, B + t)
                        pool.wait_ge(c_ready, B + t + 1)
                        carry()
                        pool.tensor_scalar(cn[:, 0:QR], csb[u][:, 0:QR], sm[:, 8:9], None, ALU.mult)
                        pool.tensor_scalar(cn[:, QR:384], csb[u][:, QR:384], sm[:, 9:10], None, ALU.mult).then_inc(cn_ready, 1)
                    if qkv:
                        ge(pool, wsq, B + t - 1)
                        ge(pool, wg_ready, B + t - 1)
                        pool.wait_ge(c_ready, B + t)
                        carry()
                        pool.tensor_copy(W4[0][:, 1, :, NOPE:QK],
                                         csb[1 - u][:, 384:CW].unsqueeze(1).to_broadcast([P, HEADS, ROPE])).then_inc(kr_ready, 1)
                        pool.wait_ge(qv_ready, B + t)
                        pool.wait_ge(k_ready, B + t)
                        pool.wait_ge(kr_ready, B + t)
                        ge(pool, qkT_ps, B + t - 1)
                        carry()
                        for z in range(2):
                            ins = pool.tensor_tensor(W4[2][:, z], W4[0][:, z], GN[:, l, z:z + 1, :].to_broadcast([P, HEADS, QK]), ALU.mult)
                        ins.then_inc(wg_ready, 1)
                mixer_steps(pool, None, step)

                DB = 0 if l == 0 else TILES
                nq = TILES if l == 0 else TILES + LAT_TILES
                pool.wait_ge(o_ready, HEADS * nq)
                pool.wait_ge(rd_in, 32 * (l + 1))

                def stage(t, u, DB=DB, t0=t0):
                    d = t + (DB - t0)
                    ge(pool, oT_ps, d)
                    carry()
                    pool.tensor_copy(Ost, ZO[:, bass.ds(t * 512, 512)]).then_inc(o_staged, 1)
                    ge(pool, op_ps, d - 1)
                    carry()
                    pool.tensor_copy(mx[u][:, 4:8, :], FT[:, :, bass.ds(t * P, P)]).then_inc(fx_ready, 1)

                def resid(t, h, u, DB=DB, t0=t0):
                    d = t + (DB - t0)
                    hh = h + (DB - t0) // 2
                    s = 1 if isinstance(t, int) and t < CTX_TILES else 0
                    pool.wait_ge(gx_ready, d + 1)
                    pool.wait_ge(xd_in[u], 16 * (hh + 1))
                    pool.tensor_tensor(xd[u], xd[u], tg, ALU.add).then_inc(x1_ready, 1)
                    pool.wait_ge(f0_ready, d + 1)
                    pool.tensor_tensor(fr[u], fr[u], rowsD[:, s, 1, :], ALU.add).then_inc(f_ready, 1)

                def dpool(t, h, u, last=False):
                    if not last:
                        stage(t + 1, 1 - u)
                    resid(t, h, u)
                stage(t0, 0)
                dpool(t0, t0 // 2, 0)
                dpool(t0 + 1, t0 // 2, 1)
                loop(pool, None, t0 + 2, TILES - 2, dpool)
                dpool(TILES - 2, TILES // 2 - 1, 0)
                dpool(TILES - 1, TILES // 2 - 1, 1, last=True)

                NB = nblocks(l)
                BB = 0 if l == 0 else nblocks(0)
                pool.wait_ge(ids_ready, l + 1)
                for u in range(2):
                    pool.wait_ge(f_out[u], 16 * (DB + TILES - t0) // 2)

                def gather(b, h, u, BB=BB):
                    hh = h + BB // 2
                    ge(pool, xg_in[u], 16 * hh)
                    ge(pool, bT_ps, BB + b - 1)
                    carry()
                    pool.tensor_copy(IDX[:, u:u + 1], IDS[:, bass.ds(b, 1)]).then_inc(idx_ready, 1)
                    pool.wait_ge(idx_ready, BB + b + 1)
                    carry()
                    pool.indirect_dma_start(xg[u], None, f_d, bass.IndirectOffsetOnAxis(ap=IDX[:, u:u + 1], axis=0)).then_inc(xg_in[u], 16)
                gather(0, 0, 0)
                gather(1, 0, 1)
                loop(pool, None, 2, NB, gather)

                pool.wait_ge(yb_ps, BB + NB)
                for u in range(2):
                    pool.wait_ge(yb_out[u], 16 * (BB + NB) // 2)

                def cg(t, h, u, DB=DB, t0=t0):
                    d = t + (DB - t0)
                    hh = h + (DB - t0) // 2
                    ge(pool, cmb, d - 1)
                    ge(pool, y_in[u], 32 * hh)
                    carry()
                    for kk in range(2):
                        pool.tensor_copy(IDX[:, 2 * kk + u:2 * kk + u + 1], DST[:, kk, bass.ds(t, 1)]).then_inc(pst_, 1)
                    pc.n += 2
                    pc.wait()
                    carry()
                    for kk, dst in enumerate((ya[u], yb[u])):
                        pool.indirect_dma_start(dst, None, yb_d, bass.IndirectOffsetOnAxis(ap=IDX[:, 2 * kk + u:2 * kk + u + 1], axis=0)
                                                ).then_inc(y_in[u], 16)
                cg.steps = 2
                if l == 0:
                    cg(0, 0, 0)
                    cg(1, 0, 1)
                loop(pool, pc, CTX_TILES, TILES, cg)
                if l == 0:
                    pool.wait_ge(cmb, TILES)

        @block.vector
        def _(dve):
            ch = Chain(dve, dst_)
            ch(dve.memset(EPSC[:], EPS))
            dve.wait_ge(cexp, 1)
            ch(dve.tensor_scalar(CE[:], CE[:], 1.0, None, ALU.add))
            ch(dve.reciprocal(CE[:], CE[:]))
            dve.tensor_tensor(CR[:], CR[:], CE[:], ALU.mult).then_inc(csilu, 1)
            dve.wait_ge(cT_ps, 1)
            dve.tensor_copy(SC[:].rearrange("p k s -> p s k"), bank(7, 0, 16).rearrange("p (s k) -> p s k", s=2)).then_inc(sc_ready, 1)
            dve.wait_ge(prm_ps, 1)
            ch(dve.tensor_copy(PCOL[:], bank(6, 0, 2 * P).rearrange("p (l n) -> p l n", l=2)[:, :, 0:67]))

            for l in range(DEPTH):
                B = TILES * l
                t0 = first_tile(l)
                dve.wait_ge(raw_ps, l + 1)
                src = bank(3, 0, 96).rearrange("p (s j) -> p s j", s=2)
                ch(dve.tensor_tensor(MOD[:, l], src, PCOL[:, l, 0:48].unsqueeze(1).to_broadcast([P, 2, 48]), ALU.add))
                for lo, w in ((8, 48), (32, 56)):
                    v = MOD[:, l, :, lo:lo + 8]
                    ch.add(dve.scalar_tensor_tensor(v, v, 1.0, PCOL[:, l, w:w + 8].unsqueeze(1).to_broadcast([P, 2, 8]), ALU.add, ALU.mult))
                ch.wait()
                dve.sem_inc(mod_done, 1)
                dve.wait_ge(rows_ps, l + 1)
                dve.tensor_copy(ROWS[:], PS[0:96, 4, 0:P]).then_inc(rows_ready, 1)

                dve.wait_ge(fm_ps, l + 1)
                dve.tensor_copy(FM[:, 0, :], bank(6))
                dve.tensor_copy(FM[:, 1, :], bank(7)).then_inc(fm_ready, 1)

                def step(t, h, u, cur=True, nxt=True, qkv=True, qt=True, B=B, l=l):
                    if nxt:
                        dve.wait_ge(xstd, B + t + 2)
                        ge(dve, xn_ready, B + t + 1)
                        dve.reciprocal(sm[:, 2:3], sm[:, 1:2]).then_inc(xrstd, 1)
                    if cur:
                        dve.wait_ge(cstd, B + t + 1)
                        ge(dve, cn_ready, B + t)
                        dve.reciprocal(sm[:, 8:10], sm[:, 6:8]).then_inc(crstd, 1)
                    if qt:
                        dve.wait_ge(qkT_ps, B + t - 1)
                        for i in range(2):
                            ins = dve.tensor_copy(kT[0:QK, 4 * i:4 * i + 4, bass.ds((t - 2) * P, P)],
                                                  PS[0:QK, 6 + i, :].rearrange("p (h n) -> p h n", h=4))
                        ins.then_inc(kT_ready, 1)
                    if nxt:
                        s = 1 if isinstance(t, int) and t + 1 < CTX_TILES else 0
                        dve.wait_ge(xT_ps, B + t + 2)
                        ge(dve, c_ps, B + t + 1)
                        for kk in range(KD):
                            ins = dve.tensor_scalar(hT[:, kk, :], bank(kk // 4, (kk % 4) * P, (kk % 4 + 1) * P),
                                                    MOD[:, l, s, 8 + kk:9 + kk], MOD[:, l, s, kk:kk + 1], ALU.mult, ALU.add)
                        ins.then_inc(hT_ready, 1)
                    if qkv:
                        dve.wait_ge(qkv_ps, B + t)
                        ge(dve, wsq, B + t - 1)
                        ge(dve, wg_ready, B + t - 1)
                        for i in range(2):
                            ins = dve.tensor_copy(W4[0][:, 1, 4 * i:4 * i + 4, 0:NOPE],
                                                  bank(6 + i).rearrange("p (h d) -> p h d", h=4)[:, :, 0:NOPE])
                        ins.then_inc(k_ready, 1)
                    if cur:
                        dve.wait_ge(cTn_ps, B + t + 1)
                        ge(dve, qkv_ps, B + t)
                        for kk in range(3):
                            ins = dve.tensor_scalar(cT[:, kk, :], bank(5, kk * P, (kk + 1) * P), PCOL[:, l, 64 + kk:65 + kk], None, ALU.mult)
                        ins.then_inc(cT_ready, 1)
                    if qkv:
                        dve.wait_ge(wsq, B + t)
                        dve.tensor_reduce(sm[:, 16:32], W3[1], AX, ALU.add).then_inc(wss, 1)
                        dve.wait_ge(wstd, B + t)
                        ch(dve.reciprocal(sm[:, 32:48], sm[:, 32:48]))
                        dve.wait_ge(wg_ready, B + t)
                        ch(dve.tensor_tensor(W3[2], W3[2], sm[:, 32:48].unsqueeze(2).to_broadcast([P, 2 * HEADS, QK]), ALU.mult))
                        rot = W3[2][:, :, NOPE:QK]
                        rcos = CST[:, bass.ds(_AT["rc"][0] + (t - 1) * ROPE, ROPE)]
                        rsin = CST[:, bass.ds(_AT["rs"][0] + (t - 1) * ROPE, ROPE)]
                        r4 = rot.rearrange("p h (a q e) -> p h a q e", a=2, q=2)
                        t4 = rt.rearrange("p (h a q e) -> p h a q e", h=2 * HEADS, a=2, q=2)
                        s4 = rsin.rearrange("p (a q e) -> p a q e", a=2, q=2)
                        for q in range(2):
                            for a in range(2):
                                ch.add(dve.tensor_tensor(t4[:, :, a, q, :], r4[:, :, a, 1 - q, :],
                                                         s4[:, a, q, :].unsqueeze(1).to_broadcast([P, 2 * HEADS, 8]), ALU.mult))
                        ch.wait()
                        ch(dve.tensor_tensor(rot, rot, rcos.unsqueeze(1).to_broadcast([P, 2 * HEADS, ROPE]), ALU.mult))
                        dve.tensor_tensor(rot, rot, rt.rearrange("p (h e) -> p h e", h=2 * HEADS), ALU.add).then_inc(wr_ready, 1)
                step.steps = 7
                mixer_steps(dve, ch, step)

                dve.wait_ge(z_ready, B + TILES)
                dve.wait_ge(qkT_ps, B + TILES)
                dve.wait_ge(q_stored, 16 * (B + TILES) + 16)
                dve.wait_ge(wg_ready, B + TILES)
                z = ZO[:, CTX_TILES * FW:]
                ch.add(dve.tensor_tensor(Fs, z[:, 0:2048], z[:, 2048:4096], ALU.add))
                ch(dve.tensor_tensor(Fd, z[:, 0:2048], z[:, 2048:4096], ALU.subtract))
                ta = z[:, 0:1024]
                ch.add(dve.tensor_tensor(ta, Fs[:, 0:1024], Fs[:, 1024:2048], ALU.add))
                ch.add(dve.tensor_tensor(Yf[:, 1024:2048], Fs[:, 0:1024], Fs[:, 1024:2048], ALU.subtract))
                ch.add(dve.tensor_tensor(z[:, 1024:1536], Fd[:, 512:1024], Fd[:, 1536:2048], ALU.subtract))
                ch(dve.tensor_tensor(z[:, 1536:2048], Fd[:, 512:1024], Fd[:, 1536:2048], ALU.add))
                ch.add(dve.tensor_tensor(Yf[:, 0:512], ta[:, 0:512], ta[:, 512:1024], ALU.add))
                ch.add(dve.tensor_tensor(Yf[:, 512:1024], ta[:, 0:512], ta[:, 512:1024], ALU.subtract))
                rh = float(np.sqrt(0.5))
                for o, src, sg, add in ((4, 1024, rh, 0), (5, 1536, rh, 1024), (6, 1024, -rh, 0)):
                    ch.add(dve.scalar_tensor_tensor(Yf[:, o * 512:(o + 1) * 512], z[:, src:src + 512], sg, Fd[:, add:add + 512], ALU.mult, ALU.add))
                ch(dve.scalar_tensor_tensor(Yf[:, 7 * 512:], z[:, 1536:2048], rh, Fd[:, 1024:1536], ALU.mult, ALU.subtract))
                dve.sem_inc(y_ready, 1)
                n = 0
                for g in range(FG):
                    for r in (0, 4, 2, 1, 3):
                        dve.wait_ge(uv_ps, 28 * l + n + 1)
                        dve.wait_ge(uv_act, 28 * l + n + 1)
                        if r not in (0, 4):
                            src = bank(n % 4, 0, 256).rearrange("p (z m) -> p z m", z=2)
                            for zz in range(2):
                                ins = dve.tensor_scalar(UV[:, zz, g, 8 - r:SEQ:8][:, ::-1], src[:, zz, :], (1.0, -1.0)[zz], None, ALU.mult)
                            ins.then_inc(uv_dve, 1)
                        n += 1
                for m in range(0, 8, 2):
                    g = m // 2
                    dve.wait_ge(ft_ps, 12 * l + m + 1)
                    ge(dve, ft_ready, 12 * l + m)
                    dve.tensor_copy(FT[:, g, CTX:CTX + 512], bank(4 + m % 4)).then_inc(ft_ready, 1)
                if l == 0:
                    dve.wait_ge(uv_ps, 20)
                    ch.add(dve.tensor_tensor(Fd[:, 0:FW], ZO[:, 0:FW], ZO[:, FW:2 * FW], ALU.add))
                    ch(dve.tensor_tensor(Fd[:, FW:2 * FW], ZO[:, 0:FW], ZO[:, FW:2 * FW], ALU.subtract))
                    dve.sem_inc(y_ready, 1)
                    for g in range(FG):
                        m = 8 + g
                        dve.wait_ge(ft_ps, m + 1)
                        dve.wait_ge(ft_ready, m)
                        dve.tensor_copy(FT[:, g, 0:CTX], bank(4 + m % 4, 0, CTX)).then_inc(ft_ready, 1)

                def vmax(n, h, nk):
                    s = HEADS * n + h
                    b = 3 * (h % 2)
                    dve.wait_ge(s_ps, s + 1)
                    ch(dve.tensor_reduce(sm[:, 48 + h % 2:49 + h % 2], PS[:, b:b + 3, :].rearrange("p b n -> p (b n)")[:, 0:nk * P], AX, ALU.max))
                    dve.tensor_scalar(sm[:, 50 + h % 2:51 + h % 2], sm[:, 48 + h % 2:49 + h % 2], -SCALE, None, ALU.mult).then_inc(nmax, 1)

                def attend(n, h, nk, tile, nxt):
                    s = HEADS * n + h
                    dve.wait_ge(p_ready, s + 1)
                    ge(dve, o_ready, s - 1)
                    dve.reciprocal(sm[:, 54 + h % 2:55 + h % 2], sm[:, 52 + h % 2:53 + h % 2]).then_inc(rinv, 1)
                    for ci in (0, 2):
                        j0, j1 = 4 * ci, min(4 * ci + 4, nk)
                        if j1 > j0:
                            dve.wait_ge(pT_ps[ci], s + 1 - (CS if ci else 0))
                            dve.tensor_copy(pT[h % 2][:, j0:j1, :].rearrange("p j n -> p (j n)"),
                                            bank(6, 0, (j1 - j0) * P)).then_inc(pT_ready[ci], 1)
                    if nxt:
                        vmax(*nxt)

                n0 = context_steps(l, attend, vmax)
                b0, c0_ = ch.base, ch.n
                with dve.Fori(0, LAT_TILES - 1) as j:
                    ch.base, ch.n = b0 + c0_ + j * HEADS, 0
                    lat_steps(attend, j + n0, j + CTX_TILES, False)
                ch.base, ch.n = b0, c0_ + (LAT_TILES - 1) * HEADS
                lat_steps(attend, n0 + LAT_TILES - 1, TILES - 1, True)

                DB = 0 if l == 0 else TILES
                dve.wait_ge(rd_in, 32 * (l + 1))

                def gated(t, u, DB=DB, t0=t0):
                    d = t + (DB - t0)
                    s = 1 if isinstance(t, int) and t < CTX_TILES else 0
                    dve.wait_ge(op_ps, d + 1)
                    ge(dve, fstd, d)
                    ge(dve, x1_ready, d)
                    dve.tensor_tensor(tg.rearrange("p (a n) -> p a n", a=2), PS[:, 2 * u:2 * u + 2, :],
                                      rowsD[:, s, 0, :].rearrange("p (a n) -> p a n", a=2), ALU.mult).then_inc(gx_ready, 1)
                    dve.wait_ge(fstd, d + 1)
                    ch(dve.reciprocal(sm[:, 2:3], sm[:, 1:2]))
                    ge(dve, rt_ps, d - 1)
                    hh = d // 2
                    ge(dve, fT_ps, d - 1)
                    return d, s

                def dvd(t, h, u, last=False, first=False, DB=DB, t0=t0):
                    if not first:
                        pass
                    d, s = gated(t, u)
                    hh = h + (DB - t0) // 2
                    ge(dve, f_out[u], 16 * hh)
                    dve.scalar_tensor_tensor(fr[u], xd[u], sm[:, 2:3], rowsD[:, s, 2, :], ALU.mult, ALU.mult).then_inc(f0_ready, 1)

                def fTevd(t, u, DB=DB, t0=t0):
                    d = t + (DB - t0)
                    dve.wait_ge(fT_ps, d + 1)
                    ge(dve, rt_ps, d)
                    dve.tensor_copy(fT[:, 4:8, :].rearrange("p k n -> p (k n)"), bank(6)).then_inc(fTd, 1)

                def ddve(t, h, u, first=False):
                    if not first:
                        fTevd(t - 1, 1 - u)
                    dvd(t, h, u)
                ddve.steps = 1
                ddve(t0, t0 // 2, 0, first=True)
                ddve(t0 + 1, t0 // 2, 1)
                loop(dve, ch, t0 + 2, TILES, ddve)
                fTevd(TILES - 1, 1)

                nt = TILES - t0
                NT = nt * NE

                def v3(a, n=NE):
                    return a[:, 0:nt * n].rearrange("p (t e) -> p t e", t=nt)

                dve.wait_ge(lexp, l + 1)
                ch(dve.tensor_scalar(SCO[:, 0:NT], LG[:, 0:NT], 1.0, None, ALU.add))
                ch(dve.reciprocal(SCO[:, 0:NT], SCO[:, 0:NT]))
                ch(dve.tensor_tensor(v3(BIA), v3(SCO), RB[:].unsqueeze(1).to_broadcast([P, nt, NE]), ALU.add))
                g4 = BIA[:, 0:NT].rearrange("p (a e) -> p a e", e=EPG)
                g6 = G6v[:, 0:nt * NG * 6].rearrange("p (a e) -> p a e", e=6)
                ch.add(dve.tensor_tensor(g6[:, :, 0:3], g4[:, :, 0:3], g4[:, :, 1:4], ALU.add))
                ch.add(dve.tensor_tensor(g6[:, :, 3:5], g4[:, :, 0:2], g4[:, :, 2:4], ALU.add))
                ch(dve.tensor_tensor(g6[:, :, 5:6], g4[:, :, 0:1], g4[:, :, 3:4], ALU.add))
                gs, gw = GSv[:, 0:nt * NG], GW[:, 0:nt * NG]
                gs3, gw3 = (a.rearrange("p (t g) -> p t g", g=NG) for a in (gs, gw))
                ch(dve.tensor_reduce(gs, g6, AX, ALU.max))

                def one_hot(dst, src, prio, n, tmp):
                    ch(dve.tensor_reduce(sm[:, 0:nt], src, AX, ALU.max))
                    mb = sm[:, 0:nt].unsqueeze(2).to_broadcast([P, nt, n])
                    ch(dve.tensor_tensor(tmp, src, mb, ALU.is_equal))
                    ch(dve.tensor_tensor(tmp, tmp, prio.unsqueeze(1).to_broadcast([P, nt, n]), ALU.mult))
                    ch(dve.tensor_reduce(sm[:, 0:nt], tmp, AX, ALU.max))
                    ch(dve.tensor_tensor(dst, tmp, mb, ALU.is_equal))
                one_hot(gw3, gs3, k("prio4"), NG, gw3)
                ch(dve.tensor_scalar(gw, gw, BIG, -BIG, ALU.mult, ALU.add))
                ch(dve.tensor_tensor(MK[:, 0:NT].rearrange("p (a e) -> p a e", e=EPG), g4,
                                     gw.unsqueeze(2).to_broadcast([P, nt * NG, EPG]), ALU.add))
                one_hot(v3(OH1), v3(MK), k("prio"), NE, v3(T1))
                ch(dve.scalar_tensor_tensor(MK[:, 0:NT], OH1[:, 0:NT], -3 * BIG, MK[:, 0:NT], ALU.mult, ALU.add))
                one_hot(v3(OH2), v3(MK), k("prio"), NE, v3(T1))
                dve.tensor_tensor(MM[:, 0:NT], OH1[:, 0:NT], OH2[:, 0:NT], ALU.add).then_inc(M_ready, 1)
                for kk, oh in enumerate((OH1, OH2)):
                    ch(dve.tensor_tensor(T1[:, 0:NT], oh[:, 0:NT], SCO[:, 0:NT], ALU.mult))
                    ch(dve.tensor_reduce(WT[:, kk, t0:TILES], v3(T1), AX, ALU.add))
                ch(dve.tensor_tensor(sm[:, 0:nt], WT[:, 0, t0:TILES], WT[:, 1, t0:TILES], ALU.add))
                ch(dve.reciprocal(sm[:, 0:nt], sm[:, 0:nt]))
                ch(dve.tensor_tensor(WT[:, :, t0:TILES], WT[:, :, t0:TILES], sm[:, 0:nt].unsqueeze(1).to_broadcast([P, 2, nt]), ALU.mult))
                dve.wait_ge(rk_ps, l + 1)
                ch(dve.tensor_copy(PRE[:, 0:NT], bank(1, 0, NT)))
                a, b, sh = PRE, PREb, NE
                while sh < NT:
                    ch.add(dve.tensor_copy(b[:, 0:sh], a[:, 0:sh]))
                    ch(dve.tensor_tensor(b[:, sh:NT], a[:, sh:NT], a[:, 0:NT - sh], ALU.add))
                    a, b, sh = b, a, 2 * sh
                ch(dve.tensor_scalar(NBL, a[:, NT - NE:NT], float(P - 1), None, ALU.add))
                ch(dve.tensor_copy(NBI, NBL))
                ch(dve.tensor_scalar(NBI, NBI, 7, None, ALU.arith_shift_right))
                ch(dve.tensor_copy(NBL, NBI))
                ch(dve.tensor_copy(PE1, NBL))
                e1, e2, sh = PE1, PE2, 1
                while sh < NE:
                    ch.add(dve.tensor_copy(e2[:, 0:sh], e1[:, 0:sh]))
                    ch(dve.tensor_tensor(e2[:, sh:NE], e1[:, sh:NE], e1[:, 0:NE - sh], ALU.add))
                    e1, e2, sh = e2, e1, 2 * sh
                ch(dve.tensor_tensor(e2, e1, NBL, ALU.subtract))
                NB = nblocks(l)
                ch(dve.tensor_scalar(USE, NBL, 1.0, None, ALU.min))
                ch(dve.tensor_copy(ORD, USE))
                o1, o2, sh = ORD, ORD2, 1
                while sh < NE:
                    ch.add(dve.tensor_copy(o2[:, 0:sh], o1[:, 0:sh]))
                    ch(dve.tensor_tensor(o2[:, sh:NE], o1[:, sh:NE], o1[:, 0:NE - sh], ALU.add))
                    o1, o2, sh = o2, o1, 2 * sh
                ch(dve.tensor_tensor(o1, o1, USE, ALU.subtract))
                cb = CB[0:1, 0:NE * NE].rearrange("p (o e) -> p o e", e=NE)
                cb2 = CB[0:1, NE * NE:2 * NE * NE].rearrange("p (o e) -> p o e", e=NE)
                iota = k("iota", 0, NE)[0:1, :]
                ch(dve.tensor_tensor(cb, o1[0:1, :].unsqueeze(1).to_broadcast([1, NE, NE]),
                                     iota.unsqueeze(2).to_broadcast([1, NE, NE]), ALU.is_equal))
                ch(dve.tensor_tensor(cb, cb, USE[0:1, :].unsqueeze(1).to_broadcast([1, NE, NE]), ALU.mult))
                ch(dve.tensor_tensor(cb2, cb, iota.unsqueeze(1).to_broadcast([1, NE, NE]), ALU.mult))
                ch(dve.tensor_reduce(CB2[0:1, 0:NE], cb2, AX, ALU.add))
                ch(dve.tensor_copy(EO[:], CB2[0:1, 0:NE]))
                ch(dve.tensor_scalar(CB2[0:1, 0:NE], e2[0:1, :], float(-NB), None, ALU.add))
                ch(dve.tensor_tensor(cb2, cb, CB2[0:1, 0:NE].unsqueeze(1).to_broadcast([1, NE, NE]), ALU.mult))
                ch(dve.tensor_reduce(CB2[0:1, 16:32], cb2, AX, ALU.add))
                ch(dve.tensor_scalar(CB2[0:1, 16:32], CB2[0:1, 16:32], float(NB), None, ALU.add))
                ch(dve.tensor_copy(FB[:], CB2[0:1, 16:32]))
                dve.sem_inc(eo_ready, 1)
                cb = CB[0:1, 0:NB * NE].rearrange("p (b e) -> p b e", e=NE)
                ch(dve.tensor_tensor(cb, CB2[0:1, 16:32].unsqueeze(1).to_broadcast([1, NB, NE]),
                                     k("iota", 0, NB)[0:1, :].unsqueeze(2).to_broadcast([1, NB, NE]), ALU.is_le))
                ch(dve.tensor_reduce(CB2[0:1, 0:NB], cb, AX, ALU.add))
                ch(dve.tensor_scalar(BE[:, 0:NB], CB2[0:1, 0:NB], -1.0, None, ALU.add))
                ch(dve.tensor_tensor(DS[:, 0:NT], a[:, 0:NT], bank(1, 0, NT), ALU.subtract))
                ch(dve.tensor_tensor(DS[:, 0:NT], DS[:, 0:NT], bank(0, 0, NT), ALU.add))
                ch(dve.scalar_tensor_tensor(v3(DS), e2.unsqueeze(1).to_broadcast([P, nt, NE]), float(P), v3(DS), ALU.mult, ALU.add))
                for kk, oh in enumerate((OH1, OH2)):
                    ch(dve.tensor_tensor(T1[:, 0:NT], oh[:, 0:NT], DS[:, 0:NT], ALU.mult))
                    ch(dve.tensor_reduce(T2[:, kk * nt:(kk + 1) * nt], v3(T1), AX, ALU.add))
                dve.tensor_copy(DST[:, :, t0:TILES], T2[:, 0:2 * nt].rearrange("p (z t) -> p z t", z=2)).then_inc(dest_ready, 1)
                ch(dve.tensor_copy(SHI_[:, 0:2 * nt], T2[:, 0:2 * nt]))
                ch(dve.tensor_scalar(SHI_[:, 0:2 * nt], SHI_[:, 0:2 * nt], 7, None, ALU.arith_shift_right))
                ch(dve.tensor_copy(SHI[:, 0:2 * nt], SHI_[:, 0:2 * nt]))
                ch(dve.scalar_tensor_tensor(SLO[:, 0:2 * nt], SHI[:, 0:2 * nt], -float(P), T2[:, 0:2 * nt], ALU.mult, ALU.add))
                for i in range(2 * nt):
                    tile = t0 + i % nt
                    dve.tensor_scalar(HOT[:, i, :], k("iota"), SLO[:, i:i + 1], None, ALU.is_equal)
                    dve.tensor_scalar(HOTB[:, i, 0:NB], k("iota", 0, NB), SHI[:, i:i + 1], k("tok", tile, tile + 1),
                                      ALU.is_equal, ALU.mult).then_inc(hot_ready, 1)
                dve.wait_ge(ids_ps, l + 1)
                dve.tensor_copy(IDS[:, 0:NB], bank(2, 0, NB)).then_inc(ids_ready, 1)

                BB = 0 if l == 0 else nblocks(0)

                def bevd(b, u, BB=BB):
                    dve.wait_ge(bT_ps, BB + b + 1)
                    ge(dve, gu_ps, BB + b - 1)
                    dve.tensor_copy(bT[u][:, 4:8, :].rearrange("p k n -> p (k n)"), bank(1)).then_inc(bTd, 1)

                def silu(b, u, BB=BB):
                    g, up = bank(2 + u, 0, DE), bank(2 + u, DE, 2 * DE)
                    dve.wait_ge(gexp, BB + b + 1)
                    ch(dve.tensor_scalar(Rs, Es, 1.0, None, ALU.add))
                    ch(dve.reciprocal(Rs, Rs))
                    ch(dve.tensor_tensor(Rs, g, Rs, ALU.mult))
                    ge(dve, aT_ps, BB + b - 1)
                    dve.tensor_tensor(aa[u], Rs, up, ALU.mult).then_inc(act_ready, 1)

                def aev(b, u, BB=BB):
                    dve.wait_ge(aT_ps, BB + b + 1)
                    ge(dve, yb_ps, BB + b)
                    dve.tensor_copy(at0, bank(4, 0, DE)).then_inc(aT_ready, 1)

                def yevd(b, h, u, BB=BB):
                    dve.wait_ge(yb_ps, BB + b + 1)
                    ge(dve, yb_out[u], 16 * (h + BB // 2))
                    dve.tensor_copy(yo[u][:, 512:D], bank(6)).then_inc(ybd, 1)
                bevd(0, 0)
                silu(0, 0)
                bevd(1, 1)
                b0, c0_ = ch.base, ch.n
                def pair(j):
                    ch.base, ch.n = b0 + c0_ + j * 6, 0
                    bevd(2 * j + 2, 0)
                    aev(2 * j, 0)
                    silu(2 * j + 1, 1)
                    yevd(2 * j, j, 0)
                    bevd(2 * j + 3, 1)
                    aev(2 * j + 1, 1)
                    silu(2 * j + 2, 0)
                    yevd(2 * j + 1, j, 1)
                pair(0)
                with dve.Fori(1, NB // 2 - 1) as j:
                    pair(j)
                ch.base, ch.n = b0, c0_ + (NB // 2 - 1) * 6
                aev(NB - 2, 0)
                silu(NB - 1, 1)
                yevd(NB - 2, NB // 2 - 1, 0)
                aev(NB - 1, 1)
                yevd(NB - 1, NB // 2 - 1, 1)

                dve.wait_ge(g2_in, 32 * (l + 1))

                def comb(t, h, u, DB=DB, t0=t0):
                    hh = h + (DB - t0) // 2
                    s = 1 if isinstance(t, int) and t < CTX_TILES else 0
                    dve.wait_ge(y_in[u], 32 * (hh + 1))
                    ch(dve.tensor_scalar(ya[u], ya[u], WT[:, 0, bass.ds(t, 1)], None, ALU.mult))
                    ch(dve.scalar_tensor_tensor(ya[u], yb[u], WT[:, 1, bass.ds(t, 1)], ya[u], ALU.mult, ALU.add))
                    ch(dve.tensor_tensor(ya[u], ya[u], G2[:, s, :], ALU.mult))
                    dve.wait_ge(xm_in[u], 16 * (hh + 1))
                    dve.tensor_tensor(xm[u], xm[u], ya[u], ALU.add).then_inc(xo_ready, 1)
                    dve.wait_ge(xo_ready, t + (DB - t0) + 1)
                    dve.sem_inc(cmb, 1)
                comb.steps = 3
                if l == 0:
                    comb(0, 0, 0)
                    comb(1, 0, 1)
                loop(dve, ch, CTX_TILES, TILES, comb)


_INS = ["x", "c", "ctx", "c_ctx", "w_ada", "b_ada", "norm_mix", "norm_ffn", "w_in", "q_a_norm", "w_q_b",
        "kv_a_norm", "w_kv_b", "q_norm", "k_norm", "w_fourier", "w_out", "router_w", "router_bias",
        "w_gate", "w_up", "w_down"]


def kernel(**inputs):
    import concourse.bacc as _bacc
    from concourse.bass_utils import run_bass_kernel_spmd as _run

    nc = _bacc.Bacc("TRN2", target_bir_lowering=False, num_devices=1)
    arrays, args = {}, []
    given = {name: np.ascontiguousarray(inputs[name]) for name in _INS}
    given["cst"] = constant_tile()
    for name, a in given.items():
        arrays[f"in_{name}"] = a
        args.append(nc.dram_tensor(f"in_{name}", a.shape, mybir.dt.from_np(a.dtype), kind="ExternalInput").ap())
    args.append(nc.dram_tensor("out_0", (1, SEQ, D), F32, kind="ExternalOutput").ap())
    build_backbone(nc, *args)
    r = _run(nc, [arrays], core_ids=[0])
    return r.results[0]["out_0"]
```

```python
from contextlib import ExitStack

import numpy as np

import concourse.bass as bass
from concourse import mybir

P = 128
D = 1024
KD = D // P
SEQ, CTX = 1024, 256
LAT_TILES, CTX_TILES = SEQ // P, CTX // P
TILES = CTX_TILES + LAT_TILES
TOK = TILES * P
DEPTH = 2
HEADS, NOPE, ROPE, VDIM = 8, 64, 32, 64
QK = NOPE + ROPE
QR, KVR = 256, 128
CW = QR + KVR + ROPE
FG, FD = 4, 128
FW = FG * FD
INW = CW + FW
GRID_W = 64
NE, NG, EPG, DE = 16, 4, 4, 256
EPS = 1e-6
SCALE = float(QK) ** -0.5
WSLOT = KD * 2 * DE + (DE // P) * D
BIG = 1e30

F32 = mybir.dt.float32
I32 = mybir.dt.int32
ALU = mybir.AluOpType
ACT = mybir.ActivationFunctionType
AX = mybir.AxisListType.X

_W = dict(ident=P, tri=P, ones=P, tw=5 * 3 * P, cc=P, nsc=P, rc=TILES * ROPE, rs=TILES * ROPE,
          prio=NE, prio4=NG, sign=2, iota=P, tok=TILES)
_AT, _n = {}, 0
for _k, _v in _W.items():
    _AT[_k] = (_n, _n + _v)
    _n += _v
CST_W = _n


def constant_tile():
    c = np.zeros((P, CST_W), np.float64)

    def put(name, a):
        c[:, _AT[name][0]:_AT[name][1]] = a

    p = np.arange(P)
    put("ident", np.eye(P))
    put("tri", (p[:, None] < p[None, :]) * 1.0)
    put("ones", 1.0)
    tw = np.zeros((P, 5, 3, P))
    for r in range(5):
        a = 2 * np.pi * ((p[:, None] * (8 * p[None, :] + r)) % SEQ) / SEQ
        tw[:, r, 0], tw[:, r, 1], tw[:, r, 2] = -np.sin(a), np.cos(a), np.sin(a)
    put("tw", tw.reshape(P, -1))
    a = 2 * np.pi * ((p[:, None] * p[None, :]) % FD) / FD
    s = 1.0 / np.sqrt(SEQ * FD)
    put("cc", np.cos(a) * s)
    put("nsc", -np.sin(a) * s)
    half = ROPE // 4
    freqs = np.float32(10000.0) ** (-np.arange(half, dtype=np.float32) / np.float32(half))
    rc = np.ones((P, TILES, ROPE))
    rs = np.zeros((P, TILES, ROPE))
    for t in range(LAT_TILES):
        n = t * P + p
        for axis, pos in enumerate((n // GRID_W, n % GRID_W)):
            ang = (pos.astype(np.float32)[:, None] * freqs).astype(np.float64)
            o = axis * 2 * half
            rc[:, CTX_TILES + t, o:o + 2 * half] = np.tile(np.cos(ang), (1, 2))
            rs[:, CTX_TILES + t, o:o + half] = -np.sin(ang)
            rs[:, CTX_TILES + t, o + half:o + 2 * half] = np.sin(ang)
    put("rc", rc.reshape(P, -1))
    put("rs", rs.reshape(P, -1))
    put("prio", np.arange(NE, 0, -1))
    put("prio4", np.arange(NG, 0, -1))
    put("iota", np.arange(P))
    put("tok", np.arange(TILES)[None, :] * P + p[:, None])
    put("sign", [1.0, -1.0])
    return c.astype(np.float32)


def build_backbone(nc, x, c, ctx, c_ctx, w_ada, b_ada, norm_mix, norm_ffn, w_in, q_a_norm, w_q_b,
                   kv_a_norm, w_kv_b, q_norm, k_norm, w_fourier, w_out, router_w, router_bias,
                   w_gate, w_up, w_down, cst, out):
    es = ExitStack()
    with es:
        def sb(name, shape, dt=F32):
            return es.enter_context(nc.sbuf_tensor(name, shape, dt))

        def sem(name):
            return es.enter_context(nc.semaphore(name))

        def dram(name, shape, dt=F32):
            return nc.dram_tensor(name, shape, dt, kind="Internal").ap()

        rows_d = dram("rows_d", (DEPTH, 2, 6 * D))
        qT_d = dram("qT_d", (TILES, QK, HEADS * P))
        xmid_d = dram("xmid_d", (TOK, D))
        xnext_d = dram("xnext_d", (TOK, D))
        f_d = dram("f_d", (TOK, D))
        NBMAX = 2 * TOK // P + NE
        yb_d = dram("yb_d", (NBMAX * P, D))

        CST = sb("CST", [P, CST_W])

        def k(name, lo=0, hi=None):
            a, b = _AT[name]
            return CST[:, a + lo:(b if hi is None else a + hi)]

        ident = k("ident")
        KV = sb("KV", [P, 15360 + 13312])
        ZO = sb("ZO", [P, TILES * FW])
        R2 = sb("R2", [P, 11776])
        PR = sb("PR", [67, DEPTH, P])
        PCOL = sb("PCOL", [P, DEPTH, 67])
        CR = sb("CR", [KD, 2, P])
        CE = sb("CE", [KD, 2, P])
        SC = sb("SC", [P, KD, 2])
        MOD = sb("MOD", [P, DEPTH, 2, 48])
        ROWS = sb("ROWS", [96, P])
        GN = sb("GN", [P, DEPTH, 2, QK])
        WF = sb("WF", [P, FG * FD])
        FM = sb("FM", [P, 2, FG * FD])
        RW = sb("RW", [P, KD, NE])
        RB = sb("RB", [P, NE])
        EPSC = sb("EPSC", [P, 1])
        sm = sb("sm", [P, 64])
        EO = sb("EO", [1, NE], I32)
        FB = sb("FB", [1, NE], I32)
        NP = sb("NP", [1, DEPTH], I32)
        BE = sb("BE", [1, NBMAX], I32)
        DST = sb("DST", [P, 2, TILES], I32)
        WT = sb("WT", [P, 2, TILES])
        IDS = sb("IDS", [P, NBMAX], I32)
        IDX = sb("IDX", [P, 4], I32)

        PS = es.enter_context(nc.psum_tensor("PS", [P, 8, 512], F32))

        def bank(b, lo=0, hi=512):
            return PS[:, b, lo:hi]

        R1 = KV[:, 15360:28672]
        kT = KV[:, 0:HEADS * TOK].rearrange("p (h n) -> p h n", h=HEADS)
        V = KV[:, 10240:15360]
        ADP = 6 * D // 512
        wada = [KV[:, o:o + 4096].rearrange("p (k n) -> p k n", k=KD) for o in (WSLOT, 2 * WSLOT, 0)]
        arow = [R2[0:2, 4096 + 512 * u:4608 + 512 * u] for u in range(3)]
        wslot = [KV[:, WSLOT * u:WSLOT * (u + 1)] for u in range(3)]
        rowsD = KV[:, 9216:15360].rearrange("p (s v n) -> p s v n", s=2, v=3)
        win = R1[:, 3328:3328 + KD * INW].rearrange("p (k n) -> p k n", k=KD)
        wqb = R1[:, 10752:12288].rearrange("p (k n) -> p k n", k=2)
        wkv = R1[:, 12288:13312]
        UV = R1[:, 0:8192].rearrange("p (z g n) -> p z g n", z=2, g=FG)
        FT = R1[:, 8192:13312].rearrange("p (g n) -> p g n", g=FG)
        wout = R1[:, 0:8192].rearrange("p (k n) -> p k n", k=KD)

        def take(sizes):
            o, views = 0, []
            for s in sizes:
                views.append(R2[:, o:o + s])
                o += s
            assert o <= 11776, o
            return views

        cst_in, cin, prm_in, gn_in = sem("cst_in"), sem("cin"), sem("prm_in"), sem("gn_in")
        cexp, csilu, cT_ps, sc_ready = sem("cexp"), sem("csilu"), sem("cT_ps"), sem("sc_ready")
        ada_in = [sem(f"ada_in{u}") for u in range(3)]
        arow_ready, arow_out, raw_in, raw_ps = sem("arow_ready"), [sem(f"arow_out{u}") for u in range(3)], sem("raw_in"), sem("raw_ps")
        ada_mm, mod_done, rows_ps, rows_ready, rows_out = (sem("ada_mm"), sem("mod_done"), sem("rows_ps"),
                                                           sem("rows_ready"), sem("rows_out"))
        prm_ps, prm_ready = sem("prm_ps"), sem("prm_ready")
        dst_ = sem("dve_step")
        ast_ = sem("act_step")
        pst_ = sem("pool_step")
        pool_turns, sp_turns = sem("pool_turns"), sem("sp_turns")
        x_in, wb_in = sem("x_in"), sem("wb_in")
        xstd, xrstd, xn_ready, xT_ps, hT_ready = sem("xstd"), sem("xrstd"), sem("xn_ready"), sem("xT_ps"), sem("hT_ready")
        z_ps, c_ps, z_ready, c_ready, cstd = sem("z_ps"), sem("c_ps"), sem("z_ready"), sem("c_ready"), sem("cstd")
        crstd, cn_ready, cTn_ps, cT_ready, qkv_ps = sem("crstd"), sem("cn_ready"), sem("cTn_ps"), sem("cT_ready"), sem("qkv_ps")
        qv_ready, k_ready, kr_ready = sem("qv_ready"), sem("k_ready"), sem("kr_ready")
        wsq, wss, wstd, wg_ready, wr_ready = sem("wsq"), sem("wss"), sem("wstd"), sem("wg_ready"), sem("wr_ready")
        qkT_ps, q_staged, kT_ready, q_stored = sem("qkT_ps"), sem("q_staged"), sem("kT_ready"), sem("q_stored")
        wf_in, fm_ps, fm_ready, y_ready = sem("wf_in"), sem("fm_ps"), sem("fm_ready"), sem("y_ready")
        uv_ps, uv_act, uv_dve, ft_ps, ft_ready = sem("uv_ps"), sem("uv_act"), sem("uv_dve"), sem("ft_ps"), sem("ft_ready")
        qs_in = [sem(f"qs_in{h}") for h in range(HEADS)]
        s_ps, nmax, p_ready, rinv, o_ps, o_ready = (sem("s_ps"), sem("nmax"), sem("p_ready"), sem("rinv"),
                                                    sem("o_ps"), sem("o_ready"))
        pT_ps = [sem(f"pT_ps{i}") for i in range(3)]
        pT_ready = [sem(f"pT_ready{i}") for i in range(3)]
        CS = CTX_TILES * HEADS
        wo_in, rd_in, xd_in = sem("wo_in"), sem("rd_in"), [sem("xd_in0"), sem("xd_in1")]
        o_staged, oT_ps, oT_ready, fx_ready, op_ps = sem("o_staged"), sem("oT_ps"), sem("oT_ready"), sem("fx_ready"), sem("op_ps")
        gx_ready, x1_ready, fstd, f0_ready, f_ready = sem("gx_ready"), sem("x1_ready"), sem("fstd"), sem("f0_ready"), sem("f_ready")
        xm_out, f_out, fT_ps, fTa, fTd, rt_ps = [sem("xm_out0"), sem("xm_out1")], [sem("f_out0"), sem("f_out1")], sem("fT_ps"), sem("fTa"), sem("fTd"), sem("rt_ps")
        rw_in, lexp, M_ready, rk_ps = sem("rw_in"), sem("lexp"), sem("M_ready"), sem("rk_ps")
        eo_ready, hot_ready, ids_ps, ids_ready = sem("eo_ready"), sem("hot_ready"), sem("ids_ps"), sem("ids_ready")
        we_in = [sem(f"we_in{u}") for u in range(3)]
        idx_ready, xg_in = sem("idx_ready"), [sem("xg_in0"), sem("xg_in1")]
        bT_ps, bTa, bTd, gu_ps, gexp, act_ready, aT_ps, aT_ready, yb_ps, yba, ybd = (
            sem("bT_ps"), sem("bTa"), sem("bTd"), sem("gu_ps"), sem("gexp"), sem("act_ready"), sem("aT_ps"),
            sem("aT_ready"), sem("yb_ps"), sem("yba"), sem("ybd"))
        yb_out = [sem("yb_out0"), sem("yb_out1")]
        g2_in, y_in, xm_in, xo_ready, xo_out = sem("g2_in"), [sem("y_in0"), sem("y_in1")], [sem("xm_in0"), sem("xm_in1")], sem("xo_ready"), [sem("xo_out0"), sem("xo_out1")]
        cmb, silu_step, yb_init, xall_in = sem("cmb"), sem("silu_step"), sem("yb_init"), sem("xall_in")

        block = es.enter_context(nc.Block())

        def ge(eng, s, v):
            if not isinstance(v, int) or v > 0:
                eng.wait_ge(s, v)

        class Chain:

            def __init__(self, eng, s):
                self.eng, self.s, self.n, self.base = eng, s, 0, 0

            def add(self, ins):
                ins.then_inc(self.s, 1)
                self.n += 1

            def wait(self):
                ge(self.eng, self.s, self.base + self.n)

            def __call__(self, ins):
                self.add(ins)
                self.wait()

        def loop(eng, chain, lo, hi, body):
            if chain is None:
                with eng.Fori(lo // 2, hi // 2) as j:
                    body(2 * j, j, 0)
                    body(2 * j + 1, j, 1)
                return
            b0, n0 = chain.base, chain.n
            per = count(chain, body)
            with eng.Fori(lo // 2, hi // 2) as j:
                chain.base = b0 + n0 + (j - lo // 2) * per
                chain.n = 0
                body(2 * j, j, 0)
                body(2 * j + 1, j, 1)
                assert chain.n == per, (chain.n, per)
            chain.base, chain.n = b0, n0 + (hi // 2 - lo // 2) * per

        def count(chain, body):
            return 2 * body.steps

        def first_step(step):
            step(-1, -1, 1, cur=False, qkv=False, qt=False)

        def mixer_steps(eng, chain, step, begun=False):
            if not begun:
                first_step(step)
            step(0, 0, 0, qkv=False, qt=False)
            step(1, 0, 1, qt=False)
            loop(eng, chain, 2, TILES - 2, step)
            step(TILES - 2, TILES // 2 - 1, 0)
            step(TILES - 1, TILES // 2 - 1, 1, nxt=False)
            step(TILES, TILES // 2, 0, cur=False, nxt=False)

        def last_step(step):
            step(TILES + 1, TILES // 2, 1, cur=False, nxt=False, qkv=False)

        def context_steps(l, attend, ahead):
            n0 = TILES * l
            tiles = [(n0 + t, CTX_TILES, t) for t in range(CTX_TILES)] if l == 0 else []
            nl = n0 + len(tiles)
            steps = [(n, h, nk, t) for n, nk, t in tiles for h in range(HEADS)]
            after = [(n, h, nk) for n, h, nk, t in steps] + [(nl, 0, TILES), (nl, 1, TILES)]
            ahead(*after[0])
            ahead(*after[1])
            for i, st in enumerate(steps):
                attend(*st, after[i + 2])
            return nl

        def lat_steps(attend, n, tile, last):
            for h in range(HEADS):
                nxt = None if last and h >= HEADS - 2 else (n + (h >= HEADS - 2), (h + 2) % HEADS, TILES)
                attend(n, h, TILES, tile, nxt)

        (xbuf, xn, hT_, c0, c1, cn, cT_, Wr, Wq, Wg, rt, qst_) = take(
            [D, D, D, CW, CW, 384, 384, 2 * HEADS * QK, 2 * HEADS * QK, 2 * HEADS * QK, 512, HEADS * P])
        csb = [c0, c1]
        hT = hT_.rearrange("p (k n) -> p k n", k=KD)
        cT = cT_.rearrange("p (k n) -> p k n", k=3)
        W4 = [w.rearrange("p (z h d) -> p z h d", z=2, h=HEADS) for w in (Wr, Wq, Wg)]
        W3 = [w.rearrange("p (h d) -> p h d", d=QK) for w in (Wr, Wq, Wg)]
        qst = qst_.rearrange("p (h n) -> p h n", h=HEADS)
        Fs, Fd = R1[:, 3328:5376], R1[:, 5376:7424]
        Fc = R2[:, 2 * D:3 * D]

        def Y(lo, hi=None):
            hi = lo + 1 if hi is None else hi
            return R2[:, lo * FW:hi * FW] if hi <= 4 else ZO[:, (CTX_TILES + lo) * FW:(CTX_TILES + hi) * FW]
        QS, p0, p1, pT0, pT1 = take([HEADS * P, TOK, TOK, TOK, TOK])
        QS = QS.rearrange("p (h n) -> p h n", h=HEADS)
        pr = [p0, p1]
        pT = [a.rearrange("p (j n) -> p j n", n=P) for a in (pT0, pT1)]
        xd0, xd1, tg, ff0, ff1, fTb, mx0, mx1, Ost = take([D, D, D, D, D, D, D, D, 512])
        xd, mx = [xd0, xd1], [a.rearrange("p (k n) -> p k n", k=KD) for a in (mx0, mx1)]
        fr = [ff0, ff1]
        fT = fTb.rearrange("p (k n) -> p k n", k=KD)
        xg0, xg1, bt0, bt1, Es, Rs, a0, a1, at0, yo0, yo1 = take([D, D, D, D, DE, DE, DE, DE, DE, D, D])
        xg, bT = [xg0, xg1], [a.rearrange("p (k n) -> p k n", k=KD) for a in (bt0, bt1)]
        aa = [a0, a1]
        aT = at0.rearrange("p (k n) -> p k n", k=2)
        yo = [yo0, yo1]
        ya0, ya1, yb0, yb1, _, G2, xm0, xm1 = take([D, D, D, D, 7424 - 4 * D, 2 * D, D, D])
        G2 = G2.rearrange("p (s n) -> p s n", s=2)
        ya, yb, xm = [ya0, ya1], [yb0, yb1], [xm0, xm1]

        def xrow(l, t, u):
            if l < DEPTH - 1:
                return xm[u]
            return KV[:, bass.ds(3 * WSLOT + (t - CTX_TILES) * D, D)]
        NT10 = TILES * NE
        (LG, SCO, BIA, MK, T1, T2, OH1, OH2, MM, PRE, PREb, DS) = take([NT10] * 12)
        G6v, GSv, GW, NBL, NBI_, PE1, PE2, CB, CB2, USE, ORD, ORD2 = [R2[:, 2048 + o:2048 + o + n] for o, n in
            ((0, 240), (240, 40), (280, 40), (320, 16), (336, 16), (352, 16), (368, 16), (384, 576), (960, 40), (1400, 16), (1416, 16), (1432, 16))]
        NBI = NBI_.bitcast(I32)
        SLO, SHI = R2[:, 3200:3200 + 2 * TILES], R2[:, 3232:3232 + 2 * TILES]
        SHI_ = R2[:, 3264:3264 + 2 * TILES].bitcast(I32)
        HOT = R2[:, 4096:4096 + 2 * TILES * P].rearrange("p (i n) -> p i n", n=P)
        HOTB = R2[:, 6656:6656 + 2 * TILES * NBMAX].rearrange("p (i n) -> p i n", n=NBMAX)

        def mirrored(n):
            return 3 * (min(n, 20) // 5) + max(0, min(n, 20) % 5 - 2)

        def first_tile(l):
            return 0 if l == 0 else CTX_TILES

        def nblocks(l):
            return 2 * (TILES - first_tile(l)) + NE

        def pairs_in_use(eng, l):
            return eng.value_load(NP[0:1, l:l + 1], min_val=nblocks(l) // 2 - NE // 2 - 2, max_val=nblocks(l) // 2 - 2) + 2

        @block.sync
        def _(sp):
            sp.sem_inc(we_in[1], 16)
            sp.sem_inc(we_in[2], 16)
            sp.sem_inc(q_stored, 16)
            sp.dma_start(CST[:], cst[:, :]).then_inc(cst_in, 16)
            sp.dma_start(CR[:, 0, :], c.rearrange("a (k n) -> (a k) n", k=KD)).then_inc(cin, 16)
            sp.dma_start(CR[:, 1, :], c_ctx.rearrange("(k n) -> k n", k=KD)).then_inc(cin, 16)
            for l in range(DEPTH):
                sp.dma_start(PR[0:48, l, :], b_ada[l].rearrange("(k n) -> k n", n=P)).then_inc(prm_in, 16)
                sp.dma_start(PR[48:56, l, :], norm_mix[l].rearrange("(k n) -> k n", n=P)).then_inc(prm_in, 16)
                sp.dma_start(PR[56:64, l, :], norm_ffn[l].rearrange("(k n) -> k n", n=P)).then_inc(prm_in, 16)
                sp.dma_start(PR[64:66, l, :], q_a_norm[l].rearrange("(k n) -> k n", n=P)).then_inc(prm_in, 16)
                sp.dma_start(PR[66:67, l, :], kv_a_norm[l].rearrange("(k n) -> k n", n=P)).then_inc(prm_in, 16)

            for l in range(DEPTH):
                sp.dma_start(GN[:, l, 0, :], q_norm[l:l + 1, :].to_broadcast([P, QK])).then_inc(gn_in, 16)
                sp.dma_start(GN[:, l, 1, :], k_norm[l:l + 1, :].to_broadcast([P, QK])).then_inc(gn_in, 16)
            sp.dma_start(RW[:], router_w.rearrange("(k p) e -> p k e", p=P)).then_inc(rw_in, 16)
            sp.dma_start(RB[:], router_bias.rearrange("(a e) -> a e", a=1).to_broadcast([P, NE])).then_inc(rw_in, 16)
            def mixer_weights(l):
                sp.dma_start(WF[:].rearrange("p (g d) -> p g d", g=FG), w_fourier[l].rearrange("g c d -> c g d")).then_inc(wf_in, 16)
                sp.dma_start(win, w_in[l].rearrange("(k p) n -> p k n", p=P)).then_inc(wb_in, 16)
                sp.dma_start(wqb, w_q_b[l].rearrange("(k p) n -> p k n", p=P)).then_inc(wb_in, 16)
                sp.dma_start(wkv, w_kv_b[l]).then_inc(wb_in, 16)

            for l in range(DEPTH):
                B = TILES * l
                t0 = first_tile(l)
                ZB = B - t0 * l

                def has_z(t, t0=t0):
                    return not isinstance(t, int) or t >= t0

                if l == 0:
                    mixer_weights(0)
                if l > 0:
                    sp.wait_ge(xo_out[0], 16 * TILES // 2)
                    sp.wait_ge(xo_out[1], 16 * TILES // 2)

                def step(t, h, u, cur=True, nxt=True, qkv=True, qt=True, l=l, B=B):
                    if nxt:
                        ge(sp, xn_ready, B + t + 1)
                        if l > 0:
                            src = xnext_d[bass.ds((t + 1) * P, P), :]
                        elif isinstance(t, int) and t + 1 < CTX_TILES:
                            src = ctx[0, (t + 1) * P:(t + 2) * P, :]
                        else:
                            src = x[0, bass.ds((t + 1 - CTX_TILES) * P, P), :]
                        sp.dma_start(xbuf, src).then_inc(x_in, 16)
                    if qt:
                        sp.wait_ge(q_staged, B + t - 1)
                        sp.dma_start(qT_d[bass.ds(t - 2, 1)].rearrange("a d n -> (a d) n"), qst_[0:QK, :]).then_inc(q_stored, 16)
                first_step(step)
                for u in range(3):
                    sp.wait_ge(arow_out[u], 16 * (ADP // 3) * (l + 1))
                if l > 0:
                    sp.wait_ge(rows_out, 16)
                sp.dma_start(ROWS[:], rows_d[l].rearrange("s (j n) -> (s j) n", n=P)).then_inc(raw_in, 16)
                sp.wait_ge(rows_ready, l + 1)
                sp.dma_start(rows_d[l].rearrange("s (j n) -> (s j) n", n=P), ROWS[:]).then_inc(rows_out, 16)
                mixer_steps(sp, None, step, begun=True)
                last_step(step)
                sp.wait_ge(q_stored, 16 * (B + TILES) + 16)

                QB = 0 if l == 0 else TILES

                def qload(n, tile, h):
                    if not isinstance(n, int) or n > QB:
                        sp.wait_ge(s_ps, HEADS * (n - 1) + h + 1)
                    sp.dma_start(QS[0:QK, h, :], qT_d[bass.ds(tile, 1), :, h * P:(h + 1) * P].rearrange("a d n -> (a d) n")
                                 ).then_inc(qs_in[h], 16)
                sp.wait_ge(y_ready, 2 if l == 0 else 3)
                sp.wait_ge(uv_ps, 28 if l == 0 else 48)
                n0 = QB
                if l == 0:
                    for t in range(CTX_TILES):
                        for h in range(HEADS):
                            qload(n0 + t, t, h)
                    n0 += CTX_TILES
                for h in range(HEADS):
                    qload(n0, CTX_TILES, h)
                sp.wait_ge(ft_ps, (12 if l == 0 else 20))
                sp.dma_start(wout, w_out[l].rearrange("(k p) n -> p k n", p=P)).then_inc(wo_in, 16)
                if l == 0:
                    for i in range(2):
                        r0 = (nblocks(0) - 2 * LAT_TILES + LAT_TILES * i) * P
                        sp.dma_start(yb_d[r0:r0 + SEQ, :], x[0]).then_inc(yb_init, 16)
                with sp.Fori(1, LAT_TILES) as j:
                    for h in range(HEADS):
                        qload(j + n0, j + CTX_TILES, h)

                sp.wait_ge(rows_out, 16 * (l + 1))
                nq = n0 + LAT_TILES
                sp.wait_ge(o_ps, HEADS * nq)
                sp.wait_ge(o_ready, HEADS * nq)
                for s in range(2):
                    sp.dma_start(rowsD[:, s].rearrange("p v n -> p (v n)"),
                                 rows_d[l, s:s + 1, 2 * D:5 * D].to_broadcast([P, 3 * D])).then_inc(rd_in, 16)

                def expert_at(o):
                    return sp.value_load(EO[0:1, bass.ds(o, 1)], min_val=0, max_val=NE - 1)

                def load_expert(e, u, l=l):
                    w = wslot[u]
                    gu = w[:, 0:KD * 2 * DE].rearrange("p (k z n) -> p k z n", k=KD, z=2)
                    for z, src in ((0, w_gate), (1, w_up)):
                        sp.dma_start(gu[:, :, z, :], src[l, bass.ds(e, 1)].rearrange("a (k p) n -> p (a k) n", p=P)
                                     ).then_inc(we_in[u], 16)
                    sp.dma_start(w[:, KD * 2 * DE:].rearrange("p (k n) -> p k n", n=D),
                                 w_down[l, bass.ds(e, 1)].rearrange("a (k p) n -> p (a k) n", p=P)).then_inc(we_in[u], 16)

                DB = 0 if l == 0 else TILES

                def dstep(t, h, u, l=l, DB=DB, t0=t0):
                    d = t + (DB - t0)
                    hh = h + (DB - t0) // 2
                    ge(sp, xm_out[u], 16 * hh)
                    if l > 0:
                        src = xnext_d[bass.ds(t * P, P), :]
                    elif isinstance(t, int) and t < CTX_TILES:
                        src = ctx[0, t * P:(t + 1) * P, :]
                    else:
                        src = x[0, bass.ds((t - CTX_TILES) * P, P), :]
                    sp.dma_start(xd[u], src).then_inc(xd_in[u], 16)

                def dstore(t, h, u, DB=DB, t0=t0):
                    d = t + (DB - t0)
                    sp.wait_ge(x1_ready, d + 1)
                    sp.dma_start(xmid_d[bass.ds(t * P, P), :], xd[u]).then_inc(xm_out[u], 16)
                    sp.wait_ge(f_ready, d + 1)
                    sp.dma_start(f_d[bass.ds(t * P, P), :], fr[u]).then_inc(f_out[u], 16)

                def dboth(t, h, u):
                    dstore(t, h, u)
                    dstep(t + 2, h + 1, u)
                dstep(t0, t0 // 2, 0)
                dstep(t0 + 1, t0 // 2, 1)
                if l == 0:
                    dboth(0, 0, 0)
                    dboth(1, 0, 1)
                loop(sp, None, CTX_TILES, TILES - 2, dboth)
                dstore(TILES - 2, TILES // 2 - 1, 0)
                dstore(TILES - 1, TILES // 2 - 1, 1)
                dn = DB + TILES - t0
                BB = 0 if l == 0 else 2 * np_
                sp.wait_ge(eo_ready, l + 1)
                np_ = pairs_in_use(sp, l)
                load_expert(expert_at(0), 0)
                e1, e2 = expert_at(1), expert_at(2)
                for u in range(2):
                    sp.wait_ge(xg_in[u], 8 * BB + 16)
                    sp.sem_inc(sp_turns, 1)
                load_expert(e1, 1)
                load_expert(e2, 2)

                def expert(e, u, BB=BB):
                    fb = sp.value_load(FB[0:1, bass.ds(e - 2, 1)], min_val=0, max_val=NBMAX)
                    real = expert_at(e)
                    sp.wait_ge(yb_ps, fb + BB)
                    load_expert(real, u)
                with sp.Fori(1, NE // 3) as j:
                    for u in range(3):
                        expert(3 * j + u, u)
                expert(NE - 1, (NE - 1) % 3)
                if l > 0:
                    for u in range(2):
                        sp.wait_ge(xm_out[u], 16 * dn // 2)
                    sp.dma_start(KV[:, 3 * WSLOT:3 * WSLOT + LAT_TILES * D].rearrange("p (t n) -> p t n", n=D),
                                 xmid_d[CTX_TILES * P:TOK, :].rearrange("(t p) n -> p t n", p=P)).then_inc(xall_in, 16)
                if l == 0:
                    mixer_weights(1)
                    for u in range(2):
                        sp.wait_ge(we_in[1 + u], 48 * 5 + 16)
                        fb = sp.value_load(FB[0:1, NE - 2 + u:NE - 1 + u], min_val=0, max_val=NBMAX)
                        sp.wait_ge(yb_ps, fb)
                        sp.sem_inc(sp_turns, 1)
                        sp.dma_start(wada[u], w_ada[1].rearrange("(k p) n -> p k n", p=P)[:, :, u * 512:(u + 1) * 512]).then_inc(ada_in[u], 16)

                def cload(t, h, u, DB=DB, t0=t0):
                    hh = h + (DB - t0) // 2
                    ge(sp, xo_out[u], 16 * hh)
                    sp.dma_start(xm[u], xmid_d[bass.ds(t * P, P), :]).then_inc(xm_in[u], 16)
                for s in range(2):
                    sp.dma_start(G2[:, s], rows_d[l, s:s + 1, 5 * D:6 * D].to_broadcast([P, D])).then_inc(g2_in, 16)
                if l == 0:
                    for u in range(2):
                        sp.wait_ge(xm_out[u], 16 * dn // 2)
                    cload(t0, t0 // 2, 0)
                    cload(t0 + 1, t0 // 2, 1)
                sp.wait_ge(yb_ps, BB + 2 * np_)
                sp.sem_inc(sp_turns, 1)
                for u in range(2):
                    sp.wait_ge(yb_out[u], 8 * BB + 16 * np_)
                    sp.sem_inc(sp_turns, 1)

                def cstore(t, h, u, DB=DB, t0=t0, l=l):
                    sp.wait_ge(xo_ready, t + (DB - t0) + 1)
                    dst = xnext_d[bass.ds(t * P, P), :] if l == 0 else out[0, bass.ds((t - CTX_TILES) * P, P), :]
                    sp.dma_start(dst, xrow(l, t, u)).then_inc(xo_out[u], 16)

                def cboth(t, h, u, l=l):
                    cstore(t, h, u)
                    if l == 0:
                        cload(t + 2, h + 1, u)
                loop(sp, None, t0, TILES - 2, cboth)
                cstore(TILES - 2, TILES // 2 - 1, 0)
                cstore(TILES - 1, TILES // 2 - 1, 1)
            dn = TILES + LAT_TILES
            sp.wait_ge(we_in[0], 48 * 6 * DEPTH)
            sp.wait_ge(we_in[1], 48 * 5 * DEPTH + 16)
            sp.wait_ge(we_in[2], 48 * 5 * DEPTH + 16)
            for u in range(2):
                sp.wait_ge(xo_out[u], 16 * dn // 2)
                sp.wait_ge(xm_out[u], 16 * dn // 2)

        @block.tensor
        def _(pe):
            pe.wait_ge(cst_in, 16)
            pe.wait_ge(prm_in, 16 * 5 * DEPTH)
            pe.wait_ge(csilu, 1)
            for s in range(2):
                mm = pe.transpose(bank(7, 8 * s, 8 * s + 8), CR[:, s, :], ident[0:KD, 0:KD])
            mm.then_inc(cT_ps, 1)
            for l in range(DEPTH):
                mm = pe.transpose(bank(6, P * l, P * l + 67), PR[:, l, :], ident[0:67, 0:67])
            mm.then_inc(prm_ps, 1)
            pe.wait_ge(sc_ready, 1)

            for l in range(DEPTH):
                B = TILES * l
                t0 = first_tile(l)
                ZB = B - t0 * l

                def has_z(t, t0=t0):
                    return not isinstance(t, int) or t >= t0

                if l > 0:
                    pe.wait_ge(yba, 2 * np_)
                    pe.wait_ge(ybd, 2 * np_)

                def ada(j, l=l):
                    for u in range(3):
                        pe.wait_ge(ada_in[u], 16 * (j + (ADP // 3 * l + 1)))
                        ge(pe, arow_ready, 3 * j + (ADP * l + u - 2))
                        for kk in range(KD):
                            mm = pe.matmul(PS[0:2, u, :], SC[:, kk, :], wada[u][:, kk, :], start=(kk == 0), stop=(kk == KD - 1))
                        mm.then_inc(ada_mm, 1)
                ada(0)
                with pe.Fori(1, ADP // 3) as j:
                    ada(j)
                pe.wait_ge(raw_in, 16 * (l + 1))
                pe.transpose(PS[:, 3, 0:96], ROWS[:], ident[0:96, 0:96]).then_inc(raw_ps, 1)
                pe.wait_ge(mod_done, l + 1)
                pe.transpose(PS[0:96, 4, 0:P], MOD[:, l].rearrange("p s j -> p (s j)"), ident).then_inc(rows_ps, 1)
                pe.wait_ge(wf_in, 16 * (l + 1))
                pe.matmul(bank(6), k("cc"), WF[:], start=True, stop=True)
                pe.matmul(bank(7), k("nsc"), WF[:], start=True, stop=True).then_inc(fm_ps, 1)
                pe.wait_ge(fm_ready, l + 1)
                pe.wait_ge(wb_in, 48 * (l + 1))
                pe.wait_ge(rows_ready, l + 1)

                def step(t, h, u, cur=True, nxt=True, qkv=True, qt=True, B=B):
                    if cur:
                        pe.wait_ge(hT_ready, B + t + 1)
                        ge(pe, cstd, B + t)
                        for kk in range(KD):
                            mm = pe.matmul(bank(2, 0, CW), hT[:, kk, :], win[:, kk, 0:CW], start=(kk == 0), stop=(kk == KD - 1))
                        mm.then_inc(c_ps, 1)
                        ge(pe, cT_ready, B + t)
                        if has_z(t):
                            for kk in range(KD):
                                mm = pe.matmul(bank(3), hT[:, kk, :], win[:, kk, CW:INW], start=(kk == 0), stop=(kk == KD - 1))
                            mm.then_inc(z_ps, 1)
                    if qt:
                        pe.wait_ge(wr_ready, B + t - 1)
                        for hh in range(2 * HEADS):
                            mm = pe.transpose(PS[0:QK, 4 + hh // 4, (hh % 4) * P:(hh % 4 + 1) * P], W3[2][:, hh, :], ident)
                        mm.then_inc(qkT_ps, 1)
                    if nxt:
                        pe.wait_ge(xn_ready, B + t + 2)
                        for kk in range(KD):
                            mm = pe.transpose(bank(kk // 4, (kk % 4) * P, (kk % 4 + 1) * P), xn[:, kk * P:(kk + 1) * P], ident)
                        mm.then_inc(xT_ps, 1)
                    if cur:
                        pe.wait_ge(cn_ready, B + t + 1)
                        if has_z(t):
                            pe.wait_ge(z_ready, ZB + t + 1)
                        for kk in range(3):
                            mm = pe.transpose(bank(3, kk * P, (kk + 1) * P), cn[:, kk * P:(kk + 1) * P], ident)
                        mm.then_inc(cTn_ps, 1)
                    if qkv:
                        pe.wait_ge(cT_ready, B + t)
                        if qt:
                            pe.wait_ge(q_staged, B + t - 1)
                            pe.wait_ge(kT_ready, B + t - 1)
                        for kk in range(2):
                            pe.matmul(bank(4, 0, 480), cT[:, kk, :], wqb[:, kk, 0:480], start=(kk == 0), stop=(kk == 1))
                        for kk in range(2):
                            pe.matmul(bank(5, 0, 288), cT[:, kk, :], wqb[:, kk, 480:768], start=(kk == 0), stop=(kk == 1))
                        pe.matmul(bank(6), cT[:, 2, :], wkv[:, 0:512], start=True, stop=True)
                        pe.matmul(bank(7), cT[:, 2, :], wkv[:, 512:1024], start=True, stop=True).then_inc(qkv_ps, 1)
                mixer_steps(pe, None, step)

                pe.wait_ge(y_ready, 1 if l == 0 else 3)
                pe.wait_ge(qv_ready, B + TILES)
                pe.wait_ge(k_ready, B + TILES)
                RES = [(0, (0,)), (4, (1,)), (2, (2, 3)), (1, (4, 5)), (3, (6, 7))]
                n = 0
                for g in range(FG):
                    for r, parts in RES:
                        if n >= 4:
                            pe.wait_ge(uv_act, 28 * l + n - 3)
                            ge(pe, uv_dve, 12 * l + mirrored(n - 3))
                        for i, part in enumerate(parts):
                            lhs = Y(part)[:, g * FD:(g + 1) * FD]
                            mm = pe.matmul(bank(n % 4, 0, 256), lhs, k("tw", r * 384 + (0 if i else P), r * 384 + (256 if i else 384)),
                                           start=(i == 0), stop=(i == len(parts) - 1))
                        mm.then_inc(uv_ps, 1)
                        n += 1
                last_step(step)
                pe.wait_ge(q_staged, B + TILES)
                pe.wait_ge(kT_ready, B + TILES)
                pe.wait_ge(uv_act, 28 * l + 20)
                ge(pe, uv_dve, 12 * l + mirrored(20))
                m = 0
                for g in range(FG):
                    for ch in range(2):
                        if m >= 4:
                            pe.wait_ge(ft_ready, (12 * l) + m - 3)
                        for z in range(2):
                            mm = pe.matmul(bank(4 + m % 4), FM[:, z, g * FD:(g + 1) * FD], UV[:, z, g, ch * 512:(ch + 1) * 512],
                                           start=(z == 0), stop=(z == 1))
                        mm.then_inc(ft_ps, 1)
                        m += 1
                if l == 0:
                    pe.wait_ge(y_ready, 2)
                    for g in range(FG):
                        for i, r in enumerate((0, 4)):
                            pe.wait_ge(uv_act, 28 * l + n - 3)
                            ge(pe, uv_dve, 12 * l + mirrored(n - 3))
                            pe.matmul(bank(n % 4, 0, 256), Fc[:, i * FW + g * FD:i * FW + (g + 1) * FD],
                                      k("tw", r * 384 + P, r * 384 + 384), start=True, stop=True).then_inc(uv_ps, 1)
                            n += 1
                    pe.wait_ge(uv_act, 28 * l + 28)
                    ge(pe, uv_dve, 12 * l + mirrored(28))
                    for g in range(FG):
                        pe.wait_ge(ft_ready, m - 3)
                        for z in range(2):
                            mm = pe.matmul(bank(4 + m % 4, 0, CTX), FM[:, z, g * FD:(g + 1) * FD], UV[:, z, g, 0:CTX],
                                           start=(z == 0), stop=(z == 1))
                        mm.then_inc(ft_ps, 1)
                        m += 1
                pe.wait_ge(ft_ready, 12 if l == 0 else 20)
                def scores(n, h, nk, parts=(0, 1, 2)):
                    b = 3 * (h % 2)
                    if 0 in parts:
                        pe.wait_ge(qs_in[h], 16 * (n + 1))
                    for i in parts:
                        w = min(512, nk * P - 512 * i)
                        if w > 0:
                            mm = pe.matmul(bank(b + i, 0, w), QS[0:QK, h, :], kT[0:QK, h, 512 * i:512 * i + w], start=True, stop=True)
                            if 512 * i + w == nk * P:
                                mm.then_inc(s_ps, 1)

                def transposes(h, nk, ci):
                    for j in range(4 * ci, min(4 * ci + 4, nk)):
                        mm = pe.transpose(bank(6 + ci % 2, (j - 4 * ci) * P, (j - 4 * ci + 1) * P), pr[h % 2][:, j * P:(j + 1) * P], ident)
                    mm.then_inc(pT_ps[ci], 1)

                def attend(n, h, nk, tile, nxt):
                    s = HEADS * n + h
                    pe.wait_ge(p_ready, s + 1)
                    transposes(h, nk, 0)
                    ge(pe, o_ready, s)
                    if nk > 4:
                        transposes(h, nk, 1)
                    if nxt:
                        scores(*nxt, parts=(0,))
                    if nk > 4:
                        pe.wait_ge(pT_ready[0], s + 1)
                        transposes(h, nk, 2)
                    if nxt:
                        scores(*nxt, parts=(1, 2))
                    for ci in range(-(-nk // 4)):
                        pe.wait_ge(pT_ready[ci], s + 1 - (CS if ci else 0))
                    for j in range(nk):
                        mm = pe.matmul(bank(7, 0, VDIM), pT[h % 2][:, j, :], V[:, j * 512 + h * VDIM:j * 512 + (h + 1) * VDIM],
                                       start=(j == 0), stop=(j == nk - 1))
                    mm.then_inc(o_ps, 1)

                n0 = context_steps(l, attend, scores)
                with pe.Fori(0, LAT_TILES - 1) as j:
                    lat_steps(attend, j + n0, j + CTX_TILES, False)
                lat_steps(attend, n0 + LAT_TILES - 1, TILES - 1, True)

                nq = n0 + LAT_TILES
                DB = 0 if l == 0 else TILES
                pe.wait_ge(o_ready, HEADS * nq)
                pe.wait_ge(wo_in, 16 * (l + 1))
                pe.wait_ge(rw_in, 32)

                def otrans(t, u, DB=DB, t0=t0):
                    d = t + (DB - t0)
                    pe.wait_ge(o_staged, d + 1)
                    ge(pe, oT_ready, d)
                    for kk in range(4):
                        mm = pe.transpose(bank(4, kk * P, (kk + 1) * P), Ost[:, kk * P:(kk + 1) * P], ident)
                    mm.then_inc(oT_ps, 1)

                def project(t, u, half, DB=DB, t0=t0):
                    d = t + (DB - t0)
                    if half == 0:
                        pe.wait_ge(oT_ready, d + 1)
                        pe.wait_ge(fx_ready, d + 1)
                        ge(pe, gx_ready, d - 1)
                    for kk in range(KD):
                        mm = pe.matmul(bank(2 * u + half), mx[u][:, kk, :], wout[:, kk, half * 512:(half + 1) * 512],
                                       start=(kk == 0), stop=(kk == KD - 1))
                    if half == 1:
                        mm.then_inc(op_ps, 1)

                def ftrans(t, u, DB=DB, t0=t0):
                    d = t + (DB - t0)
                    pe.wait_ge(f_ready, d + 1)
                    ge(pe, fTa, d)
                    ge(pe, fTd, d)
                    for kk in range(KD):
                        mm = pe.transpose(bank(5 + kk // 4, (kk % 4) * P, (kk % 4 + 1) * P), fr[u][:, kk * P:(kk + 1) * P], ident)
                    mm.then_inc(fT_ps, 1)

                def route(t, DB=DB, t0=t0):
                    d = t + (DB - t0)
                    pe.wait_ge(fTa, d + 1)
                    pe.wait_ge(fTd, d + 1)
                    for kk in range(KD):
                        mm = pe.matmul(PS[:, 7, bass.ds(t * NE, NE)], fT[:, kk, :], RW[:, kk, :], start=(kk == 0), stop=(kk == KD - 1))
                    mm.then_inc(rt_ps, 1)

                def dstep(t, h, u, routed=True, normed=True, last=False):
                    project(t, u, 0)
                    if routed:
                        route(t - 2)
                    project(t, u, 1)
                    if not last:
                        otrans(t + 1, 1 - u)
                    if normed:
                        ftrans(t - 1, 1 - u)
                otrans(t0, 0)
                dstep(t0, t0 // 2, 0, routed=False, normed=False)
                dstep(t0 + 1, t0 // 2, 1, routed=False)
                loop(pe, None, t0 + 2, TILES - 2, dstep)
                dstep(TILES - 2, 0, 0)
                dstep(TILES - 1, 0, 1, last=True)
                route(TILES - 2)
                ftrans(TILES - 1, 1)
                route(TILES - 1)

                NT = (TILES - t0) * NE
                pe.wait_ge(M_ready, l + 1)
                pe.matmul(bank(0, 0, NT), k("tri"), MM[:, 0:NT], start=True, stop=True)
                pe.matmul(bank(1, 0, NT), k("ones"), MM[:, 0:NT], start=True, stop=True).then_inc(rk_ps, 1)
                NB = nblocks(l)
                for i in range(2 * (TILES - t0)):
                    if i % 4 == 0:
                        pe.wait_ge(hot_ready, TILES // 2 * l + i // 4 + 1)
                    mm = pe.matmul(bank(2, 0, NB), HOT[:, i, :], HOTB[:, i, 0:NB], start=(i == 0), stop=(i == 2 * (TILES - t0) - 1))
                mm.then_inc(ids_ps, 1)
                pe.wait_ge(ids_ready, l + 1)

                BB = 0 if l == 0 else 2 * np_
                np_ = pairs_in_use(pe, l)

                def btrans(b, h, u, BB=BB):
                    pe.wait_ge(xg_in[u], 16 * (h + BB // 2 + 1))
                    ge(pe, bTa, BB + b)
                    ge(pe, bTd, BB + b)
                    for kk in range(KD):
                        mm = pe.transpose(bank(kk // 4, (kk % 4) * P, (kk % 4 + 1) * P), xg[u][:, kk * P:(kk + 1) * P], ident)
                    mm.then_inc(bT_ps, 1)

                def gate_up(b, e, u, BB=BB, l=l):
                    pe.wait_ge(we_in[0], (e // 3) * 48 + 48 * (6 * l + 1))
                    pe.wait_ge(we_in[1], ((e + 2) // 3) * 48 + 48 * 5 * l + 16)
                    pe.wait_ge(we_in[2], ((e + 1) // 3) * 48 + 48 * 5 * l + 16)
                    pe.wait_ge(bTa, BB + b + 1)
                    pe.wait_ge(bTd, BB + b + 1)
                    ge(pe, act_ready, BB + b - 1)
                    off = (e % 3) * WSLOT
                    for kk in range(KD):
                        mm = pe.matmul(bank(2 + u), bT[u][:, kk, :], KV[:, bass.ds(off + kk * 512, 512)],
                                       start=(kk == 0), stop=(kk == KD - 1))
                    mm.then_inc(gu_ps, 1)

                def atrans(b, u, BB=BB):
                    pe.wait_ge(act_ready, BB + b + 1)
                    ge(pe, aT_ready, BB + b)
                    for kk in range(2):
                        mm = pe.transpose(bank(4, kk * P, (kk + 1) * P), aa[u][:, kk * P:(kk + 1) * P], ident)
                    mm.then_inc(aT_ps, 1)

                def down(b, e, BB=BB):
                    pe.wait_ge(aT_ready, BB + b + 1)
                    ge(pe, yba, BB + b)
                    ge(pe, ybd, BB + b)
                    off = (e % 3) * WSLOT + KD * 2 * DE
                    for half in range(2):
                        for kk in range(2):
                            mm = pe.matmul(bank(5 + half), aT[:, kk, :], KV[:, bass.ds(off + kk * D + half * 512, 512)],
                                           start=(kk == 0), stop=(kk == 1))
                    mm.then_inc(yb_ps, 1)

                def expert_of(b):
                    return pe.value_load(BE[0:1, bass.ds(b, 1)], min_val=0, max_val=NE - 1)

                btrans(0, 0, 0)
                gate_up(0, expert_of(0), 0)
                btrans(1, 0, 1)
                def pair(j):
                    e0, e1, e2 = expert_of(2 * j), expert_of(2 * j + 1), expert_of(2 * j + 2)
                    gate_up(2 * j + 1, e1, 1)
                    atrans(2 * j, 0)
                    btrans(2 * j + 2, j + 1, 0)
                    down(2 * j, e0)
                    gate_up(2 * j + 2, e2, 0)
                    atrans(2 * j + 1, 1)
                    btrans(2 * j + 3, j + 1, 1)
                    down(2 * j + 1, e1)
                pair(0)
                with pe.Fori(1, np_ - 1) as j:
                    pair(j)
                b = 2 * np_ - 2
                e0, e1 = expert_of(b), expert_of(b + 1)
                gate_up(b + 1, e1, 1)
                atrans(b, 0)
                down(b, e0)
                atrans(b + 1, 1)
                down(b + 1, e1)

        @block.scalar
        def _(act):
            def ada_load(l, t, u):
                act.dma_start(wada[u], w_ada[l].rearrange("(k p) n -> p k n", p=P)[:, :, bass.ds(t * 512, 512)]).then_inc(ada_in[u], 16)

            act.wait_ge(cin, 32)
            for u in range(3):
                ada_load(0, u, u)
            act.wait_ge(dst_, 1)
            act.wait_ge(cin, 32)
            act.activation(CE[:], CR[:], ACT.Exp, scale=-1.0).then_inc(cexp, 1)
            for l in range(DEPTH):
                B = TILES * l
                t0 = first_tile(l)
                ZB = B - t0 * l

                def has_z(t, t0=t0):
                    return not isinstance(t, int) or t >= t0

                ch = Chain(act, ast_) if l == 0 else ch
                if l > 0:
                    act.wait_ge(yb_ps, 2 * np_)
                    act.wait_ge(we_in[0], 48 * 6)
                    ada_load(l, 2, 2)

                def ada(j, ahead, l=l):
                    for u in range(3):
                        act.wait_ge(ada_mm, 3 * j + (ADP * l + u + 1))
                        if ahead:
                            ada_load(l, 3 * j + (u + 3), u)
                        ge(act, arow_out[u], 16 * (j + ADP // 3 * l))
                        act.activation(arow[u], PS[0:2, u, :], ACT.Copy).then_inc(arow_ready, 1)
                        act.wait_ge(arow_ready, 3 * j + (ADP * l + u + 1))
                        act.dma_start(rows_d[l, :, bass.ds((3 * j + u) * 512, 512)], arow[u]).then_inc(arow_out[u], 16)
                ada(0, True)
                with act.Fori(1, ADP // 3 - 1) as j:
                    ada(j, True)
                ada(ADP // 3 - 1, False)

                def step(t, h, u, cur=True, nxt=True, qkv=True, qt=True, B=B, l=l):
                    if nxt:
                        act.wait_ge(x_in, 16 * (B + t + 2))
                        ge(act, wss, B + t - 1)
                        ge(act, xrstd, B + t + 1)
                        act.activation(Wq[:, 0:D], xbuf, ACT.Square, scale=1.0 / 32, accum_out=sm[:, 0:1]).then_inc(ast_, 1)
                        ch.n += 1
                        ch.wait()
                        act.activation(sm[:, 1:2], sm[:, 0:1], ACT.Sqrt, bias=EPSC[:, 0:1]).then_inc(xstd, 1)
                    if cur:
                        act.wait_ge(c_ps, B + t + 1)
                        ge(act, kr_ready, B + t - 1)
                        ge(act, crstd, B + t)
                        act.activation(csb[u], bank(2, 0, CW), ACT.Copy).then_inc(c_ready, 1)
                        act.activation(Wq[:, 0:QR], bank(2, 0, QR), ACT.Square, scale=1.0 / 16, accum_out=sm[:, 4:5])
                        act.activation(Wq[:, QR:QR + KVR], bank(2, QR, QR + KVR), ACT.Square, scale=float(KVR) ** -0.5,
                                       accum_out=sm[:, 5:6]).then_inc(ast_, 1)
                        ch.n += 1
                        ch.wait()
                        act.activation(sm[:, 6:8], sm[:, 4:6], ACT.Sqrt, bias=EPSC[:, 0:1]).then_inc(cstd, 1)
                        if has_z(t):
                            act.wait_ge(z_ps, ZB + t + 1)
                            act.activation(ZO[:, bass.ds(t * FW, FW)], bank(3), ACT.Copy).then_inc(z_ready, 1)
                    if qt:
                        act.wait_ge(qkT_ps, B + t - 1)
                        ge(act, q_stored, 16 * (B + t - 2) + 16)
                        act.activation(qst[0:QK, 0:4, :].rearrange("p h n -> p (h n)"), PS[0:QK, 4, :], ACT.Copy)
                        act.activation(qst[0:QK, 4:8, :].rearrange("p h n -> p (h n)"), PS[0:QK, 5, :], ACT.Copy).then_inc(q_staged, 1)
                    if qkv:
                        act.wait_ge(qkv_ps, B + t)
                        ge(act, wg_ready, B + t - 1)
                        act.activation(Wr[:, 0:480], bank(4, 0, 480), ACT.Copy).then_inc(ast_, 1)
                        act.activation(Wr[:, 480:768], bank(5, 0, 288), ACT.Copy).then_inc(ast_, 1)
                        act.wait_ge(k_ready, B + t)
                        for i in range(2):
                            ins = act.activation(V[:, bass.ds((t - 1) * 512 + i * 256, 256)].rearrange("p (h d) -> p h d", h=4),
                                                 bank(6 + i).rearrange("p (h d) -> p h d", h=4)[:, :, NOPE:], ACT.Copy)
                        ins.then_inc(qv_ready, 1)
                        ch.n += 2
                        ch.wait()
                        act.wait_ge(k_ready, B + t)
                        act.wait_ge(kr_ready, B + t)
                        act.activation(Wq, Wr, ACT.Square, scale=float(QK) ** -0.5).then_inc(wsq, 1)
                        act.wait_ge(wss, B + t)
                        act.activation(sm[:, 32:48], sm[:, 16:32], ACT.Sqrt, bias=EPSC[:, 0:1]).then_inc(wstd, 1)
                step.steps = 4
                mixer_steps(act, ch, step)

                n = 0
                for g in range(FG):
                    for r in (0, 4, 2, 1, 3):
                        act.wait_ge(uv_ps, 28 * l + n + 1)
                        act.activation(UV[:, :, g, r:SEQ:8], bank(n % 4, 0, 256).rearrange("p (z m) -> p z m", z=2),
                                       ACT.Copy).then_inc(uv_act, 1)
                        n += 1
                last_step(step)
                for m in range(8):
                    g, chk = m // 2, m % 2
                    if m % 2 == 0:
                        continue
                    act.wait_ge(ft_ps, 12 * l + m + 1)
                    act.wait_ge(ft_ready, 12 * l + m)
                    act.activation(FT[:, g, CTX + chk * 512:CTX + (chk + 1) * 512], bank(4 + m % 4), ACT.Copy).then_inc(ft_ready, 1)
                if l == 0:
                    for g in range(FG):
                        for i in range(2):
                            act.wait_ge(uv_ps, n + 1)
                            act.wait_ge(ft_ps, 8)
                            act.activation(UV[:, :, g, i:CTX:2], bank(n % 4, 0, 256).rearrange("p (z m) -> p z m", z=2),
                                           ACT.Copy, scale=2.0).then_inc(uv_act, 1)
                            n += 1

                def soft(n, h, nk):
                    s = HEADS * n + h
                    b = 3 * (h % 2)
                    act.wait_ge(nmax, s + 1)
                    act.activation(pr[h % 2][:, 0:nk * P], PS[:, b:b + 3, :].rearrange("p b n -> p (b n)")[:, 0:nk * P], ACT.Exp,
                                   bias=sm[:, 50 + h % 2:51 + h % 2], scale=SCALE, accum_out=sm[:, 52 + h % 2:53 + h % 2]
                                   ).then_inc(p_ready, 1)

                def attend(n, h, nk, tile, nxt):
                    s = HEADS * n + h
                    if nk > 4:
                        act.wait_ge(pT_ps[1], s + 1 - CS)
                        act.activation(pT[h % 2][:, 4:8, :].rearrange("p j n -> p (j n)"), bank(7), ACT.Copy).then_inc(pT_ready[1], 1)
                    act.wait_ge(rinv, s + 1)
                    act.wait_ge(o_ps, s + 1)
                    act.activation(ZO[:, bass.ds(tile * 512 + h * VDIM, VDIM)], bank(7, 0, VDIM), ACT.Copy,
                                   scale=sm[:, 54 + h % 2:55 + h % 2]).then_inc(o_ready, 1)
                    if nxt:
                        soft(*nxt)

                n0 = context_steps(l, attend, soft)
                with act.Fori(0, LAT_TILES - 1) as j:
                    lat_steps(attend, j + n0, j + CTX_TILES, False)
                lat_steps(attend, n0 + LAT_TILES - 1, TILES - 1, True)

                DB = 0 if l == 0 else TILES

                def oev(t, u, DB=DB, t0=t0):
                    d = t + (DB - t0)
                    act.wait_ge(oT_ps, d + 1)
                    ge(act, op_ps, d - 1)
                    act.activation(mx[u][:, 0:4, :].rearrange("p k n -> p (k n)"), bank(4), ACT.Copy).then_inc(oT_ready, 1)

                def frms(t, u, DB=DB, t0=t0):
                    d = t + (DB - t0)
                    act.wait_ge(x1_ready, d + 1)
                    ge(act, f0_ready, d)
                    act.activation(tg, xd[u], ACT.Square, scale=1.0 / 32, accum_out=sm[:, 0:1]).then_inc(ast_, 1)
                    ch.n += 1
                    ch.wait()
                    act.activation(sm[:, 1:2], sm[:, 0:1], ACT.Sqrt, bias=EPSC[:, 0:1]).then_inc(fstd, 1)

                def fTev(t, u, DB=DB, t0=t0):
                    d = t + (DB - t0)
                    act.wait_ge(fT_ps, d + 1)
                    ge(act, rt_ps, d)
                    act.activation(fT[:, 0:4, :].rearrange("p k n -> p (k n)"), bank(5), ACT.Copy).then_inc(fTa, 1)

                def dact(t, h, u, first=False, last=False):
                    if not last:
                        oev(t + 1, 1 - u)
                    if not first:
                        fTev(t - 1, 1 - u)
                    frms(t, u)
                dact.steps = 1
                oev(t0, 0)
                dact(t0, 0, 0, first=True)
                dact(t0 + 1, 0, 1)
                loop(act, ch, t0 + 2, TILES - 2, dact)
                dact(TILES - 2, 0, 0)
                dact(TILES - 1, 0, 1, last=True)
                fTev(TILES - 1, 1)

                NT = (TILES - t0) * NE
                DN = DB + TILES - t0
                act.wait_ge(rt_ps, DN)
                for u in range(2):
                    act.wait_ge(xm_out[u], 16 * DN // 2)
                    act.wait_ge(f_out[u], 16 * DN // 2)
                act.activation(LG[:, 0:NT], bank(7, t0 * NE, TILES * NE), ACT.Exp, scale=-1.0).then_inc(lexp, 1)

                BB = 0 if l == 0 else 2 * np_
                act.wait_ge(ids_ready, l + 1)
                act.wait_ge(yb_init, 32)
                np_ = pairs_in_use(act, l)

                def bev(b, u, BB=BB):
                    act.wait_ge(bT_ps, BB + b + 1)
                    ge(act, gu_ps, BB + b - 1)
                    act.activation(bT[u][:, 0:4, :].rearrange("p k n -> p (k n)"), bank(0), ACT.Copy).then_inc(bTa, 1)

                def gev(b, u, BB=BB):
                    act.wait_ge(gu_ps, BB + b + 1)
                    ge(act, act_ready, BB + b)
                    act.activation(Es, bank(2 + u, 0, DE), ACT.Exp, scale=-1.0).then_inc(gexp, 1)

                def yev(b, h, u, BB=BB):
                    act.wait_ge(yb_ps, BB + b + 1)
                    ge(act, yb_out[u], 16 * (h + BB // 2))
                    act.activation(yo[u][:, 0:512], bank(5), ACT.Copy).then_inc(yba, 1)
                    act.wait_ge(yba, BB + b + 1)
                    act.wait_ge(ybd, BB + b + 1)
                    act.dma_start(yb_d[bass.ds(b * P, P), :], yo[u]).then_inc(yb_out[u], 16)
                bev(0, 0)
                gev(0, 0)
                bev(1, 1)
                def pair(j):
                    gev(2 * j + 1, 1)
                    bev(2 * j + 2, 0)
                    yev(2 * j, j, 0)
                    gev(2 * j + 2, 0)
                    bev(2 * j + 3, 1)
                    yev(2 * j + 1, j, 1)
                pair(0)
                with act.Fori(1, np_ - 1) as j:
                    pair(j)
                gev(2 * np_ - 1, 1)
                yev(2 * np_ - 2, np_ - 1, 0)
                yev(2 * np_ - 1, np_ - 1, 1)

        @block.gpsimd
        def _(pool):
            def carry():
                pool.sem_inc(pool_turns, 1)

            pc = Chain(pool, pst_)
            for l in range(DEPTH):
                B = TILES * l
                t0 = first_tile(l)
                ZB = B - t0 * l

                def has_z(t, t0=t0):
                    return not isinstance(t, int) or t >= t0

                if l == 0:
                    pool.wait_ge(gn_in, 16 * 2 * DEPTH)

                def step(t, h, u, cur=True, nxt=True, qkv=True, qt=True, B=B, l=l):
                    if nxt:
                        pool.wait_ge(xrstd, B + t + 2)
                        ge(pool, xT_ps, B + t + 1)
                        pool.wait_ge(x_in, 16 * (B + t + 2))
                        carry()
                        pool.tensor_scalar(xn, xbuf, sm[:, 2:3], None, ALU.mult).then_inc(xn_ready, 1)
                    if cur:
                        pool.wait_ge(crstd, B + t + 1)
                        ge(pool, cTn_ps, B + t)
                        pool.wait_ge(c_ready, B + t + 1)
                        carry()
                        pool.tensor_scalar(cn[:, 0:QR], csb[u][:, 0:QR], sm[:, 8:9], None, ALU.mult)
                        pool.tensor_scalar(cn[:, QR:384], csb[u][:, QR:384], sm[:, 9:10], None, ALU.mult).then_inc(cn_ready, 1)
                    if qkv:
                        ge(pool, wsq, B + t - 1)
                        ge(pool, wg_ready, B + t - 1)
                        pool.wait_ge(c_ready, B + t)
                        carry()
                        pool.tensor_copy(W4[0][:, 1, :, NOPE:QK],
                                         csb[1 - u][:, 384:CW].unsqueeze(1).to_broadcast([P, HEADS, ROPE])).then_inc(kr_ready, 1)
                        pool.wait_ge(qv_ready, B + t)
                        pool.wait_ge(k_ready, B + t)
                        pool.wait_ge(kr_ready, B + t)
                        ge(pool, qkT_ps, B + t - 1)
                        carry()
                        for z in range(2):
                            ins = pool.tensor_tensor(W4[2][:, z], W4[0][:, z], GN[:, l, z:z + 1, :].to_broadcast([P, HEADS, QK]), ALU.mult)
                        ins.then_inc(wg_ready, 1)
                mixer_steps(pool, None, step)

                DB = 0 if l == 0 else TILES
                pool.wait_ge(o_ready, HEADS * (TILES * l + 1))

                def stage(t, u, DB=DB, t0=t0):
                    d = t + (DB - t0)
                    ge(pool, oT_ps, d)
                    carry()
                    pool.tensor_copy(Ost, ZO[:, bass.ds(t * 512, 512)]).then_inc(o_staged, 1)
                    ge(pool, op_ps, d - 1)
                    carry()
                    pool.tensor_copy(mx[u][:, 4:8, :], FT[:, :, bass.ds(t * P, P)]).then_inc(fx_ready, 1)

                def resid(t, h, u, DB=DB, t0=t0):
                    d = t + (DB - t0)
                    hh = h + (DB - t0) // 2
                    s = 1 if isinstance(t, int) and t < CTX_TILES else 0
                    pool.wait_ge(gx_ready, d + 1)
                    pool.wait_ge(xd_in[u], 16 * (hh + 1))
                    pool.tensor_tensor(xd[u], xd[u], tg, ALU.add).then_inc(x1_ready, 1)
                    pool.wait_ge(f0_ready, d + 1)
                    pool.tensor_tensor(fr[u], fr[u], rowsD[:, s, 1, :], ALU.add).then_inc(f_ready, 1)

                def dpool(t, h, u, last=False):
                    if not last:
                        stage(t + 1, 1 - u)
                    resid(t, h, u)
                stage(t0, 0)
                pool.wait_ge(o_ready, HEADS * (TILES if l == 0 else TILES + LAT_TILES))
                pool.wait_ge(rd_in, 32 * (l + 1))
                dpool(t0, t0 // 2, 0)
                dpool(t0 + 1, t0 // 2, 1)
                loop(pool, None, t0 + 2, TILES - 2, dpool)
                dpool(TILES - 2, TILES // 2 - 1, 0)
                dpool(TILES - 1, TILES // 2 - 1, 1, last=True)

                BB = 0 if l == 0 else 2 * np_
                pool.wait_ge(ids_ready, l + 1)
                np_ = pairs_in_use(pool, l)
                for u in range(2):
                    pool.wait_ge(f_out[u], 16 * (DB + TILES - t0) // 2)

                def gather(b, h, u, BB=BB):
                    hh = h + BB // 2
                    ge(pool, xg_in[u], 16 * hh)
                    ge(pool, bT_ps, BB + b - 1)
                    carry()
                    pool.tensor_copy(IDX[:, u:u + 1], IDS[:, bass.ds(b, 1)]).then_inc(idx_ready, 1)
                    pool.wait_ge(idx_ready, BB + b + 1)
                    carry()
                    pool.indirect_dma_start(xg[u], None, f_d, bass.IndirectOffsetOnAxis(ap=IDX[:, u:u + 1], axis=0)).then_inc(xg_in[u], 16)
                gather(0, 0, 0)
                gather(1, 0, 1)
                with pool.Fori(1, np_) as j:
                    for u in range(2):
                        gather(2 * j + u, j, u)

                pool.wait_ge(yb_ps, BB + 2 * np_)
                for u in range(2):
                    pool.wait_ge(yb_out[u], 8 * BB + 16 * np_)
                    carry()

                def cg(t, h, u, DB=DB, t0=t0):
                    d = t + (DB - t0)
                    hh = h + (DB - t0) // 2
                    ge(pool, cmb, d - 1)
                    ge(pool, y_in[u], 32 * hh)
                    carry()
                    for kk in range(2):
                        pool.tensor_copy(IDX[:, 2 * kk + u:2 * kk + u + 1], DST[:, kk, bass.ds(t, 1)]).then_inc(pst_, 1)
                    pc.n += 2
                    pc.wait()
                    carry()
                    for kk, dst in enumerate((ya[u], yb[u])):
                        pool.indirect_dma_start(dst, None, yb_d, bass.IndirectOffsetOnAxis(ap=IDX[:, 2 * kk + u:2 * kk + u + 1], axis=0)
                                                ).then_inc(y_in[u], 16)
                cg.steps = 2
                if l == 0:
                    cg(0, 0, 0)
                    cg(1, 0, 1)
                loop(pool, pc, CTX_TILES, TILES, cg)
                if l == 0:
                    pool.wait_ge(cmb, TILES)

        @block.vector
        def _(dve):
            ch = Chain(dve, dst_)
            ch(dve.memset(EPSC[:], EPS))
            dve.wait_ge(cexp, 1)
            ch(dve.tensor_scalar(CE[:], CE[:], 1.0, None, ALU.add))
            ch(dve.reciprocal(CE[:], CE[:]))
            dve.tensor_tensor(CR[:], CR[:], CE[:], ALU.mult).then_inc(csilu, 1)
            dve.wait_ge(cT_ps, 1)
            dve.tensor_copy(SC[:].rearrange("p k s -> p s k"), bank(7, 0, 16).rearrange("p (s k) -> p s k", s=2)).then_inc(sc_ready, 1)
            dve.wait_ge(prm_ps, 1)
            ch(dve.tensor_copy(PCOL[:], bank(6, 0, 2 * P).rearrange("p (l n) -> p l n", l=2)[:, :, 0:67]))

            for l in range(DEPTH):
                B = TILES * l
                t0 = first_tile(l)
                ZB = B - t0 * l

                def has_z(t, t0=t0):
                    return not isinstance(t, int) or t >= t0

                dve.wait_ge(raw_ps, l + 1)
                src = bank(3, 0, 96).rearrange("p (s j) -> p s j", s=2)
                ch(dve.tensor_tensor(MOD[:, l], src, PCOL[:, l, 0:48].unsqueeze(1).to_broadcast([P, 2, 48]), ALU.add))
                for lo, w in ((8, 48), (32, 56)):
                    v = MOD[:, l, :, lo:lo + 8]
                    ch.add(dve.scalar_tensor_tensor(v, v, 1.0, PCOL[:, l, w:w + 8].unsqueeze(1).to_broadcast([P, 2, 8]), ALU.add, ALU.mult))
                ch.wait()
                dve.sem_inc(mod_done, 1)
                dve.wait_ge(rows_ps, l + 1)
                dve.tensor_copy(ROWS[:], PS[0:96, 4, 0:P]).then_inc(rows_ready, 1)

                dve.wait_ge(fm_ps, l + 1)
                dve.tensor_copy(FM[:, 0, :], bank(6))
                dve.tensor_copy(FM[:, 1, :], bank(7)).then_inc(fm_ready, 1)

                def dft(B=B, l=l):
                    dve.wait_ge(z_ready, ZB + TILES)
                    dve.wait_ge(xT_ps, B + TILES)
                    z = ZO[:, CTX_TILES * FW:]
                    ch.add(dve.tensor_tensor(Fs, z[:, 0:2048], z[:, 2048:4096], ALU.add))
                    ch(dve.tensor_tensor(Fd, z[:, 0:2048], z[:, 2048:4096], ALU.subtract))
                    ta = z[:, 0:1024]
                    ch.add(dve.tensor_tensor(ta, Fs[:, 0:1024], Fs[:, 1024:2048], ALU.add))
                    ch.add(dve.tensor_tensor(Y(2, 4), Fs[:, 0:1024], Fs[:, 1024:2048], ALU.subtract))
                    ch.add(dve.tensor_tensor(z[:, 1024:1536], Fd[:, 512:1024], Fd[:, 1536:2048], ALU.subtract))
                    ch(dve.tensor_tensor(z[:, 1536:2048], Fd[:, 512:1024], Fd[:, 1536:2048], ALU.add))
                    ch.add(dve.tensor_tensor(Y(0), ta[:, 0:512], ta[:, 512:1024], ALU.add))
                    ch.add(dve.tensor_tensor(Y(1), ta[:, 0:512], ta[:, 512:1024], ALU.subtract))
                    rh = float(np.sqrt(0.5))
                    for o, src, sg, add in ((4, 1024, rh, 0), (5, 1536, rh, 1024), (6, 1024, -rh, 0)):
                        ch.add(dve.scalar_tensor_tensor(Y(o), z[:, src:src + 512], sg, Fd[:, add:add + 512], ALU.mult, ALU.add))
                    ch(dve.scalar_tensor_tensor(Y(7), z[:, 1536:2048], rh, Fd[:, 1024:1536], ALU.mult, ALU.subtract))
                    dve.sem_inc(y_ready, 1)
                    if l == 0:
                        ch.add(dve.tensor_tensor(Fc[:, 0:FW], ZO[:, 0:FW], ZO[:, FW:2 * FW], ALU.add))
                        ch(dve.tensor_tensor(Fc[:, FW:2 * FW], ZO[:, 0:FW], ZO[:, FW:2 * FW], ALU.subtract))
                        dve.sem_inc(y_ready, 1)

                def step(t, h, u, cur=True, nxt=True, qkv=True, qt=True, B=B, l=l):
                    if nxt:
                        dve.wait_ge(xstd, B + t + 2)
                        ge(dve, xn_ready, B + t + 1)
                        dve.reciprocal(sm[:, 2:3], sm[:, 1:2]).then_inc(xrstd, 1)
                    if cur:
                        dve.wait_ge(cstd, B + t + 1)
                        ge(dve, cn_ready, B + t)
                        dve.reciprocal(sm[:, 8:10], sm[:, 6:8]).then_inc(crstd, 1)
                    if qt:
                        dve.wait_ge(qkT_ps, B + t - 1)
                        for i in range(2):
                            ins = dve.tensor_copy(kT[0:QK, 4 * i:4 * i + 4, bass.ds((t - 2) * P, P)],
                                                  PS[0:QK, 6 + i, :].rearrange("p (h n) -> p h n", h=4))
                        ins.then_inc(kT_ready, 1)
                    if nxt:
                        s = 1 if isinstance(t, int) and t + 1 < CTX_TILES else 0
                        dve.wait_ge(xT_ps, B + t + 2)
                        ge(dve, c_ps, B + t + 1)
                        if has_z(t):
                            ge(dve, z_ps, ZB + t + 1)
                        for kk in range(KD):
                            ins = dve.tensor_scalar(hT[:, kk, :], bank(kk // 4, (kk % 4) * P, (kk % 4 + 1) * P),
                                                    MOD[:, l, s, 8 + kk:9 + kk], MOD[:, l, s, kk:kk + 1], ALU.mult, ALU.add)
                        ins.then_inc(hT_ready, 1)
                    if qkv:
                        dve.wait_ge(qkv_ps, B + t)
                        ge(dve, wsq, B + t - 1)
                        ge(dve, wg_ready, B + t - 1)
                        for i in range(2):
                            ins = dve.tensor_copy(W4[0][:, 1, 4 * i:4 * i + 4, 0:NOPE],
                                                  bank(6 + i).rearrange("p (h d) -> p h d", h=4)[:, :, 0:NOPE])
                        ins.then_inc(k_ready, 1)
                        if isinstance(t, int) and t == TILES:
                            dft()
                    if cur:
                        dve.wait_ge(cTn_ps, B + t + 1)
                        ge(dve, qkv_ps, B + t)
                        for kk in range(3):
                            ins = dve.tensor_scalar(cT[:, kk, :], bank(3, kk * P, (kk + 1) * P), PCOL[:, l, 64 + kk:65 + kk], None, ALU.mult)
                        ins.then_inc(cT_ready, 1)
                    if qkv:
                        dve.wait_ge(wsq, B + t)
                        dve.tensor_reduce(sm[:, 16:32], W3[1], AX, ALU.add).then_inc(wss, 1)
                        dve.wait_ge(wstd, B + t)
                        ch(dve.reciprocal(sm[:, 32:48], sm[:, 32:48]))
                        dve.wait_ge(wg_ready, B + t)
                        ch(dve.tensor_tensor(W3[2], W3[2], sm[:, 32:48].unsqueeze(2).to_broadcast([P, 2 * HEADS, QK]), ALU.mult))
                        rot = W3[2][:, :, NOPE:QK]
                        rcos = CST[:, bass.ds(_AT["rc"][0] + (t - 1) * ROPE, ROPE)]
                        rsin = CST[:, bass.ds(_AT["rs"][0] + (t - 1) * ROPE, ROPE)]
                        r4 = rot.rearrange("p h (a q e) -> p h a q e", a=2, q=2)
                        t4 = rt.rearrange("p (h a q e) -> p h a q e", h=2 * HEADS, a=2, q=2)
                        s4 = rsin.rearrange("p (a q e) -> p a q e", a=2, q=2)
                        for q in range(2):
                            for a in range(2):
                                ch.add(dve.tensor_tensor(t4[:, :, a, q, :], r4[:, :, a, 1 - q, :],
                                                         s4[:, a, q, :].unsqueeze(1).to_broadcast([P, 2 * HEADS, 8]), ALU.mult))
                        ch.wait()
                        ch(dve.tensor_tensor(rot, rot, rcos.unsqueeze(1).to_broadcast([P, 2 * HEADS, ROPE]), ALU.mult))
                        dve.tensor_tensor(rot, rot, rt.rearrange("p (h e) -> p h e", h=2 * HEADS), ALU.add).then_inc(wr_ready, 1)
                step.steps = 7
                mixer_steps(dve, ch, step)

                n = 0
                for g in range(FG):
                    for r in (0, 4, 2, 1, 3):
                        dve.wait_ge(uv_ps, 28 * l + n + 1)
                        dve.wait_ge(uv_act, 28 * l + n + 1)
                        if r not in (0, 4):
                            src = bank(n % 4, 0, 256).rearrange("p (z m) -> p z m", z=2)
                            for zz in range(2):
                                ins = dve.tensor_scalar(UV[:, zz, g, 8 - r:SEQ:8][:, ::-1], src[:, zz, :], (1.0, -1.0)[zz], None, ALU.mult)
                            ins.then_inc(uv_dve, 1)
                        n += 1
                last_step(step)
                for m in range(0, 8, 2):
                    g = m // 2
                    dve.wait_ge(ft_ps, 12 * l + m + 1)
                    ge(dve, ft_ready, 12 * l + m)
                    dve.tensor_copy(FT[:, g, CTX:CTX + 512], bank(4 + m % 4)).then_inc(ft_ready, 1)
                if l == 0:
                    for g in range(FG):
                        m = 8 + g
                        dve.wait_ge(ft_ps, m + 1)
                        dve.wait_ge(ft_ready, m)
                        dve.tensor_copy(FT[:, g, 0:CTX], bank(4 + m % 4, 0, CTX)).then_inc(ft_ready, 1)

                def vmax(n, h, nk):
                    s = HEADS * n + h
                    b = 3 * (h % 2)
                    dve.wait_ge(s_ps, s + 1)
                    ch(dve.tensor_reduce(sm[:, 48 + h % 2:49 + h % 2], PS[:, b:b + 3, :].rearrange("p b n -> p (b n)")[:, 0:nk * P], AX, ALU.max))
                    dve.tensor_scalar(sm[:, 50 + h % 2:51 + h % 2], sm[:, 48 + h % 2:49 + h % 2], -SCALE, None, ALU.mult).then_inc(nmax, 1)

                def attend(n, h, nk, tile, nxt):
                    s = HEADS * n + h
                    dve.wait_ge(p_ready, s + 1)
                    ge(dve, o_ready, s - 1)
                    dve.reciprocal(sm[:, 54 + h % 2:55 + h % 2], sm[:, 52 + h % 2:53 + h % 2]).then_inc(rinv, 1)
                    for ci in (0, 2):
                        j0, j1 = 4 * ci, min(4 * ci + 4, nk)
                        if j1 > j0:
                            dve.wait_ge(pT_ps[ci], s + 1 - (CS if ci else 0))
                            dve.tensor_copy(pT[h % 2][:, j0:j1, :].rearrange("p j n -> p (j n)"),
                                            bank(6, 0, (j1 - j0) * P)).then_inc(pT_ready[ci], 1)
                    if nxt:
                        vmax(*nxt)

                n0 = context_steps(l, attend, vmax)
                b0, c0_ = ch.base, ch.n
                with dve.Fori(0, LAT_TILES - 1) as j:
                    ch.base, ch.n = b0 + c0_ + j * HEADS, 0
                    lat_steps(attend, j + n0, j + CTX_TILES, False)
                ch.base, ch.n = b0, c0_ + (LAT_TILES - 1) * HEADS
                lat_steps(attend, n0 + LAT_TILES - 1, TILES - 1, True)

                DB = 0 if l == 0 else TILES
                dve.wait_ge(rd_in, 32 * (l + 1))

                def gated(t, u, DB=DB, t0=t0):
                    d = t + (DB - t0)
                    s = 1 if isinstance(t, int) and t < CTX_TILES else 0
                    dve.wait_ge(op_ps, d + 1)
                    ge(dve, fstd, d)
                    ge(dve, x1_ready, d)
                    dve.tensor_tensor(tg.rearrange("p (a n) -> p a n", a=2), PS[:, 2 * u:2 * u + 2, :],
                                      rowsD[:, s, 0, :].rearrange("p (a n) -> p a n", a=2), ALU.mult).then_inc(gx_ready, 1)
                    dve.wait_ge(fstd, d + 1)
                    ch(dve.reciprocal(sm[:, 2:3], sm[:, 1:2]))
                    ge(dve, fT_ps, d - 1)
                    return d, s

                def dvd(t, h, u, DB=DB, t0=t0):
                    d, s = gated(t, u)
                    hh = h + (DB - t0) // 2
                    ge(dve, f_out[u], 16 * hh)
                    dve.scalar_tensor_tensor(fr[u], xd[u], sm[:, 2:3], rowsD[:, s, 2, :], ALU.mult, ALU.mult).then_inc(f0_ready, 1)

                def fTevd(t, u, DB=DB, t0=t0):
                    d = t + (DB - t0)
                    dve.wait_ge(fT_ps, d + 1)
                    ge(dve, rt_ps, d)
                    dve.tensor_copy(fT[:, 4:8, :].rearrange("p k n -> p (k n)"), bank(6)).then_inc(fTd, 1)

                def ddve(t, h, u, first=False):
                    if not first:
                        fTevd(t - 1, 1 - u)
                    dvd(t, h, u)
                ddve.steps = 1
                ddve(t0, t0 // 2, 0, first=True)
                ddve(t0 + 1, t0 // 2, 1)
                loop(dve, ch, t0 + 2, TILES, ddve)
                fTevd(TILES - 1, 1)

                nt = TILES - t0
                NT = nt * NE

                def v3(a, n=NE):
                    return a[:, 0:nt * n].rearrange("p (t e) -> p t e", t=nt)

                dve.wait_ge(lexp, l + 1)
                ch(dve.tensor_scalar(SCO[:, 0:NT], LG[:, 0:NT], 1.0, None, ALU.add))
                ch(dve.reciprocal(SCO[:, 0:NT], SCO[:, 0:NT]))
                ch(dve.tensor_tensor(v3(BIA), v3(SCO), RB[:].unsqueeze(1).to_broadcast([P, nt, NE]), ALU.add))
                g4 = BIA[:, 0:NT].rearrange("p (a e) -> p a e", e=EPG)
                g6 = G6v[:, 0:nt * NG * 6].rearrange("p (a e) -> p a e", e=6)
                ch.add(dve.tensor_tensor(g6[:, :, 0:3], g4[:, :, 0:3], g4[:, :, 1:4], ALU.add))
                ch.add(dve.tensor_tensor(g6[:, :, 3:5], g4[:, :, 0:2], g4[:, :, 2:4], ALU.add))
                ch(dve.tensor_tensor(g6[:, :, 5:6], g4[:, :, 0:1], g4[:, :, 3:4], ALU.add))
                gs, gw = GSv[:, 0:nt * NG], GW[:, 0:nt * NG]
                gs3, gw3 = (a.rearrange("p (t g) -> p t g", g=NG) for a in (gs, gw))
                ch(dve.tensor_reduce(gs, g6, AX, ALU.max))

                def one_hot(dst, src, prio, n, tmp):
                    ch(dve.tensor_reduce(sm[:, 0:nt], src, AX, ALU.max))
                    mb = sm[:, 0:nt].unsqueeze(2).to_broadcast([P, nt, n])
                    ch(dve.tensor_tensor(tmp, src, mb, ALU.is_equal))
                    ch(dve.tensor_tensor(tmp, tmp, prio.unsqueeze(1).to_broadcast([P, nt, n]), ALU.mult))
                    ch(dve.tensor_reduce(sm[:, 0:nt], tmp, AX, ALU.max))
                    ch(dve.tensor_tensor(dst, tmp, mb, ALU.is_equal))
                one_hot(gw3, gs3, k("prio4"), NG, gw3)
                ch(dve.tensor_scalar(gw, gw, BIG, -BIG, ALU.mult, ALU.add))
                ch(dve.tensor_tensor(MK[:, 0:NT].rearrange("p (a e) -> p a e", e=EPG), g4,
                                     gw.unsqueeze(2).to_broadcast([P, nt * NG, EPG]), ALU.add))
                one_hot(v3(OH1), v3(MK), k("prio"), NE, v3(T1))
                ch(dve.scalar_tensor_tensor(MK[:, 0:NT], OH1[:, 0:NT], -3 * BIG, MK[:, 0:NT], ALU.mult, ALU.add))
                one_hot(v3(OH2), v3(MK), k("prio"), NE, v3(T1))
                dve.tensor_tensor(MM[:, 0:NT], OH1[:, 0:NT], OH2[:, 0:NT], ALU.add).then_inc(M_ready, 1)
                dve.wait_ge(rk_ps, l + 1)
                ch(dve.tensor_copy(PRE[:, 0:NT], bank(1, 0, NT)))
                a, b, sh = PRE, PREb, NE
                while sh < NT:
                    ch.add(dve.tensor_copy(b[:, 0:sh], a[:, 0:sh]))
                    ch(dve.tensor_tensor(b[:, sh:NT], a[:, sh:NT], a[:, 0:NT - sh], ALU.add))
                    a, b, sh = b, a, 2 * sh
                ch(dve.tensor_scalar(NBL, a[:, NT - NE:NT], float(P - 1), None, ALU.add))
                ch(dve.tensor_copy(NBI, NBL))
                ch(dve.tensor_scalar(NBI, NBI, 7, None, ALU.arith_shift_right))
                ch(dve.tensor_copy(NBL, NBI))
                ch(dve.tensor_copy(PE1, NBL))
                e1, e2, sh = PE1, PE2, 1
                while sh < NE:
                    ch.add(dve.tensor_copy(e2[:, 0:sh], e1[:, 0:sh]))
                    ch(dve.tensor_tensor(e2[:, sh:NE], e1[:, sh:NE], e1[:, 0:NE - sh], ALU.add))
                    e1, e2, sh = e2, e1, 2 * sh
                ch(dve.tensor_tensor(e2, e1, NBL, ALU.subtract))
                NB = nblocks(l)
                ch(dve.tensor_scalar(USE, NBL, 1.0, None, ALU.min))
                ch(dve.tensor_copy(ORD, USE))
                o1, o2, sh = ORD, ORD2, 1
                while sh < NE:
                    ch.add(dve.tensor_copy(o2[:, 0:sh], o1[:, 0:sh]))
                    ch(dve.tensor_tensor(o2[:, sh:NE], o1[:, sh:NE], o1[:, 0:NE - sh], ALU.add))
                    o1, o2, sh = o2, o1, 2 * sh
                ch(dve.tensor_tensor(o1, o1, USE, ALU.subtract))
                cb = CB[0:1, 0:NE * NE].rearrange("p (o e) -> p o e", e=NE)
                cb2 = CB[0:1, NE * NE:2 * NE * NE].rearrange("p (o e) -> p o e", e=NE)
                iota = k("iota", 0, NE)[0:1, :]
                ch(dve.tensor_tensor(cb, o1[0:1, :].unsqueeze(1).to_broadcast([1, NE, NE]),
                                     iota.unsqueeze(2).to_broadcast([1, NE, NE]), ALU.is_equal))
                ch(dve.tensor_tensor(cb, cb, USE[0:1, :].unsqueeze(1).to_broadcast([1, NE, NE]), ALU.mult))
                ch(dve.tensor_tensor(cb2, cb, iota.unsqueeze(1).to_broadcast([1, NE, NE]), ALU.mult))
                ch(dve.tensor_reduce(CB2[0:1, 0:NE], cb2, AX, ALU.add))
                ch(dve.tensor_copy(EO[:], CB2[0:1, 0:NE]))
                ch(dve.tensor_scalar(CB2[0:1, 0:NE], e2[0:1, :], float(-NB), None, ALU.add))
                ch(dve.tensor_tensor(cb2, cb, CB2[0:1, 0:NE].unsqueeze(1).to_broadcast([1, NE, NE]), ALU.mult))
                ch(dve.tensor_reduce(CB2[0:1, 16:32], cb2, AX, ALU.add))
                ch(dve.tensor_scalar(CB2[0:1, 16:32], CB2[0:1, 16:32], float(NB), None, ALU.add))
                ch(dve.tensor_tensor(CB2[0:1, 0:NE], CB2[0:1, 16:32], e1[0:1, NE - 1:NE].to_broadcast([1, NE]), ALU.min))
                ch(dve.tensor_copy(FB[:], CB2[0:1, 0:NE]))
                ch(dve.tensor_scalar(CB2[0:1, 0:1], e1[0:1, NE - 1:NE], -3.0, None, ALU.add))
                ch(dve.tensor_copy(NP[:, l:l + 1], CB2[0:1, 0:1]))
                ch(dve.tensor_scalar(NP[:, l:l + 1], NP[:, l:l + 1], 1, None, ALU.arith_shift_right))
                dve.sem_inc(eo_ready, 1)
                ch(dve.tensor_tensor(DS[:, 0:NT], a[:, 0:NT], bank(1, 0, NT), ALU.subtract))
                ch(dve.tensor_tensor(DS[:, 0:NT], DS[:, 0:NT], bank(0, 0, NT), ALU.add))
                ch(dve.scalar_tensor_tensor(v3(DS), e2.unsqueeze(1).to_broadcast([P, nt, NE]), float(P), v3(DS), ALU.mult, ALU.add))
                for kk, oh in enumerate((OH1, OH2)):
                    ch(dve.tensor_tensor(T1[:, 0:NT], oh[:, 0:NT], DS[:, 0:NT], ALU.mult))
                    ch(dve.tensor_reduce(T2[:, kk * nt:(kk + 1) * nt], v3(T1), AX, ALU.add))
                ch.add(dve.tensor_copy(DST[:, :, t0:TILES], T2[:, 0:2 * nt].rearrange("p (z t) -> p z t", z=2)))
                ch(dve.tensor_copy(SHI_[:, 0:2 * nt], T2[:, 0:2 * nt]))
                ch(dve.tensor_scalar(SHI_[:, 0:2 * nt], SHI_[:, 0:2 * nt], 7, None, ALU.arith_shift_right))
                ch(dve.tensor_copy(SHI[:, 0:2 * nt], SHI_[:, 0:2 * nt]))
                ch(dve.scalar_tensor_tensor(SLO[:, 0:2 * nt], SHI[:, 0:2 * nt], -float(P), T2[:, 0:2 * nt], ALU.mult, ALU.add))
                hb = HOTB[:, 0:2 * nt, 0:NB]
                ch(dve.tensor_tensor(hb, k("iota", 0, NB).unsqueeze(1).to_broadcast([P, 2 * nt, NB]),
                                     SHI[:, 0:2 * nt].unsqueeze(2).to_broadcast([P, 2 * nt, NB]), ALU.is_equal))
                for kk in range(2):
                    ch.add(dve.tensor_tensor(hb[:, kk * nt:(kk + 1) * nt, :], hb[:, kk * nt:(kk + 1) * nt, :],
                                             k("tok", t0, TILES).unsqueeze(2).to_broadcast([P, nt, NB]), ALU.mult))
                ch.wait()
                for i in range(0, 2 * nt, 4):
                    dve.tensor_tensor(HOT[:, i:i + 4, :], k("iota").unsqueeze(1).to_broadcast([P, 4, P]),
                                      SLO[:, i:i + 4].unsqueeze(2).to_broadcast([P, 4, P]), ALU.is_equal).then_inc(hot_ready, 1)
                cb = CB[0:1, 0:NB * NE].rearrange("p (b e) -> p b e", e=NE)
                ch(dve.tensor_tensor(cb, CB2[0:1, 16:32].unsqueeze(1).to_broadcast([1, NB, NE]),
                                     k("iota", 0, NB)[0:1, :].unsqueeze(2).to_broadcast([1, NB, NE]), ALU.is_le))
                ch(dve.tensor_reduce(CB2[0:1, 0:NB], cb, AX, ALU.add))
                ch(dve.tensor_scalar(BE[:, 0:NB], CB2[0:1, 0:NB], -1.0, None, ALU.add))
                for kk, oh in enumerate((OH1, OH2)):
                    ch(dve.tensor_tensor(T1[:, 0:NT], oh[:, 0:NT], SCO[:, 0:NT], ALU.mult))
                    ch(dve.tensor_reduce(WT[:, kk, t0:TILES], v3(T1), AX, ALU.add))
                ch(dve.tensor_tensor(sm[:, 0:nt], WT[:, 0, t0:TILES], WT[:, 1, t0:TILES], ALU.add))
                ch(dve.reciprocal(sm[:, 0:nt], sm[:, 0:nt]))
                ch(dve.tensor_tensor(WT[:, :, t0:TILES], WT[:, :, t0:TILES], sm[:, 0:nt].unsqueeze(1).to_broadcast([P, 2, nt]), ALU.mult))
                dve.wait_ge(ids_ps, l + 1)
                dve.tensor_copy(IDS[:, 0:NB], bank(2, 0, NB)).then_inc(ids_ready, 1)

                BB = 0 if l == 0 else 2 * np_
                np_ = pairs_in_use(dve, l)
                sc = Chain(dve, silu_step)
                sc.base = 3 * BB

                def bevd(b, u, BB=BB):
                    dve.wait_ge(bT_ps, BB + b + 1)
                    ge(dve, gu_ps, BB + b - 1)
                    dve.tensor_copy(bT[u][:, 4:8, :].rearrange("p k n -> p (k n)"), bank(1)).then_inc(bTd, 1)

                def silu(b, u, BB=BB):
                    g, up = bank(2 + u, 0, DE), bank(2 + u, DE, 2 * DE)
                    dve.wait_ge(gexp, BB + b + 1)
                    sc(dve.tensor_scalar(Rs, Es, 1.0, None, ALU.add))
                    sc(dve.reciprocal(Rs, Rs))
                    sc(dve.tensor_tensor(Rs, g, Rs, ALU.mult))
                    ge(dve, aT_ps, BB + b - 1)
                    dve.tensor_tensor(aa[u], Rs, up, ALU.mult).then_inc(act_ready, 1)

                def aev(b, u, BB=BB):
                    dve.wait_ge(aT_ps, BB + b + 1)
                    ge(dve, yb_ps, BB + b)
                    dve.tensor_copy(at0, bank(4, 0, DE)).then_inc(aT_ready, 1)

                def yevd(b, h, u, BB=BB):
                    dve.wait_ge(yb_ps, BB + b + 1)
                    ge(dve, yb_out[u], 16 * (h + BB // 2))
                    dve.tensor_copy(yo[u][:, 512:D], bank(6)).then_inc(ybd, 1)
                bevd(0, 0)
                silu(0, 0)
                bevd(1, 1)
                def pair(j):
                    sc.base, sc.n = 3 * BB + 6 * j, 3
                    aev(2 * j, 0)
                    bevd(2 * j + 2, 0)
                    silu(2 * j + 1, 1)
                    yevd(2 * j, j, 0)
                    aev(2 * j + 1, 1)
                    bevd(2 * j + 3, 1)
                    silu(2 * j + 2, 0)
                    yevd(2 * j + 1, j, 1)
                pair(0)
                with dve.Fori(1, np_ - 1) as j:
                    pair(j)
                sc.base, sc.n = 3 * BB + 6 * np_, -3
                aev(2 * np_ - 2, 0)
                silu(2 * np_ - 1, 1)
                yevd(2 * np_ - 2, np_ - 1, 0)
                aev(2 * np_ - 1, 1)
                yevd(2 * np_ - 1, np_ - 1, 1)

                dve.wait_ge(g2_in, 32 * (l + 1))

                if l > 0:
                    dve.wait_ge(xall_in, 16)

                def comb(t, h, u, DB=DB, t0=t0, l=l):
                    hh = h + (DB - t0) // 2
                    s = 1 if isinstance(t, int) and t < CTX_TILES else 0
                    dve.wait_ge(y_in[u], 32 * (hh + 1))
                    ch(dve.tensor_scalar(ya[u], ya[u], WT[:, 0, bass.ds(t, 1)], None, ALU.mult))
                    ch(dve.scalar_tensor_tensor(ya[u], yb[u], WT[:, 1, bass.ds(t, 1)], ya[u], ALU.mult, ALU.add))
                    ch(dve.tensor_tensor(ya[u], ya[u], G2[:, s, :], ALU.mult))
                    if l == 0:
                        dve.wait_ge(xm_in[u], 16 * (hh + 1))
                    dve.tensor_tensor(xrow(l, t, u), xrow(l, t, u), ya[u], ALU.add).then_inc(xo_ready, 1)
                    dve.wait_ge(xo_ready, t + (DB - t0) + 1)
                    dve.sem_inc(cmb, 1)
                comb.steps = 3
                if l == 0:
                    comb(0, 0, 0)
                    comb(1, 0, 1)
                loop(dve, ch, CTX_TILES, TILES, comb)


_INS = ["x", "c", "ctx", "c_ctx", "w_ada", "b_ada", "norm_mix", "norm_ffn", "w_in", "q_a_norm", "w_q_b",
        "kv_a_norm", "w_kv_b", "q_norm", "k_norm", "w_fourier", "w_out", "router_w", "router_bias",
        "w_gate", "w_up", "w_down"]


def kernel(**inputs):
    import concourse.bacc as _bacc
    from concourse.bass_utils import run_bass_kernel_spmd as _run

    nc = _bacc.Bacc("TRN2", target_bir_lowering=False, num_devices=1)
    arrays, args = {}, []
    given = {name: np.ascontiguousarray(inputs[name]) for name in _INS}
    given["cst"] = constant_tile()
    for name, a in given.items():
        arrays[f"in_{name}"] = a
        args.append(nc.dram_tensor(f"in_{name}", a.shape, mybir.dt.from_np(a.dtype), kind="ExternalInput").ap())
    args.append(nc.dram_tensor("out_0", (1, SEQ, D), F32, kind="ExternalOutput").ap())
    build_backbone(nc, *args)
    r = _run(nc, [arrays], core_ids=[0])
    return r.results[0]["out_0"]
```
